# Optimizing a Trainium2 kernel written in Bass

```python
import math
import jax
import jax.numpy as jnp
from jax import lax
import numpy as np

D_MODEL = 1024
BATCH = 1
SEQ = 256
DEPTH = 2

PLE_DIM = 256
D_FF = 2816
EPS = 1e-6
Q_BLOCK = 128

A_HEADS = 8
A_HEAD_DIM = 64
MOBA_BLOCK = 256
MOBA_TOPK = 3
MOBA_Q_CHUNK = 16

B_HEADS = 8
MLA_Q_RANK = 256
MLA_KV_RANK = 128
MLA_NOPE = 64
MLA_ROPE = 32
MLA_V = 64
ROPE_THETA = 10000.0

T5_BUCKETS = 32
T5_MAX_DIST = 128

C_HEADS = 16
C_HEAD_DIM = 64

A_WIDTH = A_HEADS * A_HEAD_DIM
B_WIDTH = B_HEADS * MLA_V
AB_IN = 3 * A_WIDTH + MLA_Q_RANK + MLA_KV_RANK + MLA_ROPE
AB_OUT = A_WIDTH + B_WIDTH
C_WIDTH = C_HEADS * C_HEAD_DIM
C_IN = 3 * C_WIDTH + C_HEADS
N_EVEN = (DEPTH + 1) // 2
N_ODD = DEPTH // 2

kernel_name = 'hybrid_moba_mla_fox_macaron'

F32 = jnp.float32

def rmsnorm(x, g):
    xf = x.astype(F32)
    y = xf * lax.rsqrt(jnp.mean(xf * xf, axis=-1, keepdims=True) + EPS)
    return (y * g.astype(F32)).astype(x.dtype)

def swiglu(h, w_in, w_out):
    a, u = jnp.split(h @ w_in, 2, axis=-1)
    return (jax.nn.silu(a) * u) @ w_out

def split_heads(t, n_heads):
    b, s, _ = t.shape
    return t.reshape(b, s, n_heads, -1).transpose(0, 2, 1, 3)

def merge_heads(t):
    b, h, s, d = t.shape
    return t.transpose(0, 2, 1, 3).reshape(b, s, h * d)

def rope(x, pos):
    half = x.shape[-1] // 2
    inv = ROPE_THETA ** (-jnp.arange(half, dtype=F32) / half)
    ang = pos[:, None] * inv[None, :]
    cos, sin = jnp.cos(ang), jnp.sin(ang)
    xf = x.astype(F32)
    x1, x2 = xf[..., :half], xf[..., half:]
    return jnp.concatenate([x1 * cos - x2 * sin, x1 * sin + x2 * cos], axis=-1).astype(x.dtype)

def t5_bucket(dist):
    dist = jnp.maximum(dist, 0)
    max_exact = T5_BUCKETS // 2
    d = jnp.maximum(dist.astype(F32), 1.0)
    large = max_exact + (jnp.log(d / max_exact) / math.log(T5_MAX_DIST / max_exact)
                         * (T5_BUCKETS - max_exact)).astype(jnp.int32)
    large = jnp.minimum(large, T5_BUCKETS - 1)
    return jnp.where(dist < max_exact, dist, large)

def causal_block_attention(q, k, v, scale, log_decay_cum=None):
    b, h, s, dq = q.shape
    dv = v.shape[-1]
    nq = s // Q_BLOCK
    qb = q.reshape(b, h, nq, Q_BLOCK, dq).transpose(2, 0, 1, 3, 4)
    key_pos = jnp.arange(s)

    def block_fn(xs):
        i, q_i = xs[0], xs[1]
        logits = jnp.einsum('bhqd,bhkd->bhqk', q_i, k).astype(F32) * scale
        if log_decay_cum is not None:
            c_i = xs[2]
            logits = logits + (c_i[..., :, None] - log_decay_cum[..., None, :])
        q_pos = i * Q_BLOCK + jnp.arange(Q_BLOCK)
        mask = key_pos[None, :] <= q_pos[:, None]
        probs = jax.nn.softmax(jnp.where(mask, logits, -jnp.inf), axis=-1)
        return jnp.einsum('bhqk,bhkd->bhqd', probs.astype(v.dtype), v)

    xs = (jnp.arange(nq), qb)
    if log_decay_cum is not None:
        xs = xs + (log_decay_cum.reshape(b, h, nq, Q_BLOCK).transpose(2, 0, 1, 3),)
    out = lax.map(block_fn, xs)
    return out.transpose(1, 2, 0, 3, 4).reshape(b, h, s, dv)

def moba_attention(q, k, v, t5_table):
    b, h, s, dh = q.shape
    nb = -(-s // MOBA_BLOCK)
    pad = nb * MOBA_BLOCK - s
    k_blk = jnp.pad(k, ((0, 0), (0, 0), (0, pad), (0, 0))).reshape(b, h, nb, MOBA_BLOCK, dh)
    v_blk = jnp.pad(v, ((0, 0), (0, 0), (0, pad), (0, 0))).reshape(b, h, nb, MOBA_BLOCK, dh)
    pos = jnp.arange(s)
    own = (pos // MOBA_BLOCK).astype(jnp.int32)
    n_sel = min(MOBA_TOPK, nb - 1)
    own_idx = jnp.broadcast_to(own[:, None], (b, h, s, 1))
    if n_sel > 0:
        k_mean = k_blk.astype(F32).mean(axis=3)
        gate = jnp.einsum('bhsd,bhnd->bhsn', q.astype(F32), k_mean)
        past = jnp.arange(nb)[None, :] < own[:, None]
        gate = jnp.where(past, gate, -jnp.inf)
        _, top_idx = lax.top_k(gate, n_sel)
        sel_idx = jnp.concatenate([top_idx.astype(jnp.int32), own_idx], axis=-1)
        sel_valid = jnp.concatenate([jnp.arange(n_sel)[None, :] < own[:, None],
                                     jnp.ones((s, 1), dtype=bool)], axis=-1)
    else:
        sel_idx = own_idx
        sel_valid = jnp.ones((s, 1), dtype=bool)
    n_slots = n_sel + 1
    nqc = s // MOBA_Q_CHUNK
    qc = q.reshape(b, h, nqc, MOBA_Q_CHUNK, dh).transpose(2, 0, 1, 3, 4)
    idxc = sel_idx.reshape(b, h, nqc, MOBA_Q_CHUNK, n_slots).transpose(2, 0, 1, 3, 4)
    validc = sel_valid.reshape(nqc, MOBA_Q_CHUNK, n_slots)
    table_h = t5_table.T.astype(F32)
    bi = jnp.arange(b)[:, None, None, None]
    hi4 = jnp.arange(h)[None, :, None, None]
    hi5 = jnp.arange(h)[None, :, None, None, None]
    scale = dh ** -0.5

    def chunk_fn(xs):
        ci, q_i, idx_i, valid_i = xs
        k_g = k_blk[bi, hi4, idx_i]
        v_g = v_blk[bi, hi4, idx_i]
        logits = jnp.einsum('bhqd,bhqnkd->bhqnk', q_i, k_g).astype(F32) * scale
        q_pos = ci * MOBA_Q_CHUNK + jnp.arange(MOBA_Q_CHUNK)
        k_pos = idx_i[..., None] * MOBA_BLOCK + jnp.arange(MOBA_BLOCK)
        dist = q_pos[None, None, :, None, None] - k_pos
        bias = table_h[hi5, t5_bucket(dist)]
        mask = (dist >= 0) & valid_i[None, None, :, :, None]
        logits = jnp.where(mask, logits + bias, -jnp.inf)
        probs = jax.nn.softmax(logits.reshape(b, h, MOBA_Q_CHUNK, n_slots * MOBA_BLOCK), axis=-1)
        probs = probs.reshape(b, h, MOBA_Q_CHUNK, n_slots, MOBA_BLOCK)
        return jnp.einsum('bhqnk,bhqnkd->bhqd', probs.astype(v.dtype), v_g)

    out = lax.map(chunk_fn, (jnp.arange(nqc), qc, idxc, validc))
    return out.transpose(1, 2, 0, 3, 4).reshape(b, h, s, dh)

def mla_attention(cq, ckv, kr, q_norm, w_uq, kv_norm, w_ukv):
    b, s, _ = cq.shape
    pos = jnp.arange(s, dtype=F32)
    q = split_heads(rmsnorm(cq, q_norm) @ w_uq, B_HEADS)
    kv = split_heads(rmsnorm(ckv, kv_norm) @ w_ukv, B_HEADS)
    q_full = jnp.concatenate([q[..., :MLA_NOPE], rope(q[..., MLA_NOPE:], pos)], axis=-1)
    k_rope = jnp.broadcast_to(rope(kr, pos)[:, None], (b, B_HEADS, s, MLA_ROPE))
    k_full = jnp.concatenate([kv[..., :MLA_NOPE], k_rope], axis=-1)
    v = kv[..., MLA_NOPE:]
    return causal_block_attention(q_full, k_full, v, (MLA_NOPE + MLA_ROPE) ** -0.5)

def moba_mla_mixer(h, w_in, t5_table, q_norm, w_uq, kv_norm, w_ukv, w_out):
    u = h @ w_in
    cuts = np.cumsum([A_WIDTH, A_WIDTH, A_WIDTH, MLA_Q_RANK, MLA_KV_RANK]).tolist()
    qa, ka, va, cq, ckv, kr = jnp.split(u, cuts, axis=-1)
    oa = moba_attention(split_heads(qa, A_HEADS), split_heads(ka, A_HEADS),
                        split_heads(va, A_HEADS), t5_table)
    ob = mla_attention(cq, ckv, kr, q_norm, w_uq, kv_norm, w_ukv)
    return jnp.concatenate([merge_heads(oa), merge_heads(ob)], axis=-1) @ w_out

def fox_mixer(h, w_in, b_f, w_out):
    u = h @ w_in
    q, k, v, f = jnp.split(u, [C_WIDTH, 2 * C_WIDTH, 3 * C_WIDTH], axis=-1)
    log_f = jax.nn.log_sigmoid((f + b_f).astype(F32))
    cum = jnp.cumsum(log_f, axis=1).transpose(0, 2, 1)
    o = causal_block_attention(split_heads(q, C_HEADS), split_heads(k, C_HEADS),
                               split_heads(v, C_HEADS), C_HEAD_DIM ** -0.5, cum)
    return merge_heads(o) @ w_out

def setup_inputs(seed: int = 0) -> dict:
    key = jax.random.key(seed)
    ks = iter(jax.random.split(key, 32))

    def w(shape, fan_in):
        return jax.random.normal(next(ks), shape, F32) * fan_in ** -0.5

    def gain(shape):
        return 1.0 + 0.02 * jax.random.normal(next(ks), shape, F32)

    return {
        'x': jax.random.normal(next(ks), (BATCH, SEQ, D_MODEL), F32),
        'p': jax.random.normal(next(ks), (DEPTH, BATCH, SEQ, PLE_DIM), F32),
        't5_bias': 0.5 * jax.random.normal(next(ks), (T5_BUCKETS, A_HEADS), F32),
        'ff1_norm': gain((DEPTH, D_MODEL)),
        'ff1_w_in': w((DEPTH, D_MODEL, 2 * D_FF), D_MODEL),
        'ff1_w_out': w((DEPTH, D_FF, D_MODEL), D_FF),
        'mix_norm': gain((DEPTH, D_MODEL)),
        'ff2_norm': gain((DEPTH, D_MODEL)),
        'ff2_w_in': w((DEPTH, D_MODEL, 2 * D_FF), D_MODEL),
        'ff2_w_out': w((DEPTH, D_FF, D_MODEL), D_FF),
        'ple_norm': gain((DEPTH, D_MODEL)),
        'ple_w_gate': w((DEPTH, D_MODEL, D_MODEL), D_MODEL),
        'ple_w_proj': w((DEPTH, PLE_DIM, D_MODEL), PLE_DIM),
        'ab_w_in': w((N_EVEN, D_MODEL, AB_IN), D_MODEL),
        'mla_q_norm': gain((N_EVEN, MLA_Q_RANK)),
        'mla_w_uq': w((N_EVEN, MLA_Q_RANK, B_HEADS * (MLA_NOPE + MLA_ROPE)), MLA_Q_RANK),
        'mla_kv_norm': gain((N_EVEN, MLA_KV_RANK)),
        'mla_w_ukv': w((N_EVEN, MLA_KV_RANK, B_HEADS * (MLA_NOPE + MLA_V)), MLA_KV_RANK),
        'ab_w_out': w((N_EVEN, AB_OUT, D_MODEL), AB_OUT),
        'fox_w_in': w((N_ODD, D_MODEL, C_IN), D_MODEL),
        'fox_b_f': 3.0 + 0.5 * jax.random.normal(next(ks), (N_ODD, C_HEADS), F32),
        'fox_w_out': w((N_ODD, C_WIDTH, D_MODEL), C_WIDTH),
        'final_norm': gain((D_MODEL,)),
    }

def reference(x, p, t5_bias, ff1_norm, ff1_w_in, ff1_w_out, mix_norm, ff2_norm, ff2_w_in,
              ff2_w_out, ple_norm, ple_w_gate, ple_w_proj, ab_w_in, mla_q_norm, mla_w_uq,
              mla_kv_norm, mla_w_ukv, ab_w_out, fox_w_in, fox_b_f, fox_w_out, final_norm):
    for i in range(DEPTH):
        x = x + 0.5 * swiglu(rmsnorm(x, ff1_norm[i]), ff1_w_in[i], ff1_w_out[i])
        h = rmsnorm(x, mix_norm[i])
        j = i // 2
        if i % 2 == 0:
            x = x + moba_mla_mixer(h, ab_w_in[j], t5_bias, mla_q_norm[j], mla_w_uq[j],
                                   mla_kv_norm[j], mla_w_ukv[j], ab_w_out[j])
        else:
            x = x + fox_mixer(h, fox_w_in[j], fox_b_f[j], fox_w_out[j])
        x = x + 0.5 * swiglu(rmsnorm(x, ff2_norm[i]), ff2_w_in[i], ff2_w_out[i])
        g = jax.nn.sigmoid(rmsnorm(x, ple_norm[i]) @ ple_w_gate[i])
        x = x + g * (p[i] @ ple_w_proj[i])
    return rmsnorm(x, final_norm)


_drawn_inputs = setup_inputs


def setup_inputs(seed=0):
    import zlib

    import numpy as np

    out = dict(_drawn_inputs(seed))
    spreads = {}
    factors = {'ff1_norm': 5.525,
     'mix_norm': 5.899,
     'ff2_norm': 5.978,
     'ple_norm': 8.0,
     'mla_q_norm': 8.0,
     'mla_kv_norm': 8.0,
     'final_norm': 2.828}
    for name, (base, spread) in spreads.items():
        noise = np.random.default_rng([zlib.crc32(name.encode()), seed]).standard_normal(out[name].shape)
        drawn = base * np.exp(spread * noise) if base else spread * noise
        out[name] = jnp.asarray(drawn.astype(out[name].dtype))
    for name, factor in factors.items():
        out[name] = (out[name] * factor).astype(out[name].dtype)
    return out
```

```python
import concourse.bass as bass
from concourse import mybir
from concourse.alu_op_type import AluOpType as ALU
from contextlib import ExitStack

P = 128
T = 2
SEQ = T * P
D = 1024
KD = D // P
FF = 2816
PAIRS = FF // 256
LAYERS = 2
RING = 3
UNIT = 2048
HALF = UNIT // 2
EPS = 1e-6
A_HEADS, A_DIM = 8, 64
B_HEADS, NOPE, ROPE, VDIM = 8, 64, 32, 64
Q_RANK, KV_RANK = 256, 128
QK_B = NOPE + ROPE
C_HEADS, C_DIM = 16, 64
AUG = 2
MLA_C = Q_RANK + KV_RANK + ROPE
HEADS = 16
BIG = 3.0e38

FFN_UNITS = 3 * PAIRS
AB1 = D
AB2 = 3 * A_HEADS * A_DIM + MLA_C - D
WIDTHS = []
START = {}


def _lay_out_units():
    def phase(name, widths):
        START[name] = len(WIDTHS)
        WIDTHS.extend(widths)
    for layer in range(LAYERS):
        phase(("ffn", 2 * layer), [UNIT] * FFN_UNITS)
        if layer == 0:
            phase("ab1", [2 * AB1] * 4)
            phase("ab2", [2 * AB2] * 4)
            phase("uq", [2 * B_HEADS * QK_B])
            phase("ukv", [B_HEADS * (NOPE + VDIM)])
        else:
            phase("fox_q", [UNIT] * 4)
            phase("fox_k", [UNIT] * 4)
            phase("fox_v", [UNIT] * 4)
            phase("fox_f", [KD * C_HEADS])
        phase(("out", layer), [UNIT] * 4)
        phase(("ffn", 2 * layer + 1), [UNIT] * FFN_UNITS)
        phase(("proj", layer), [UNIT])
        phase(("gate", layer), [UNIT] * 4)


_lay_out_units()
N_UNITS = len(WIDTHS)


def program(nc, x_in, p_in, t5_bias, ff1_norm, ff1_w_in, ff1_w_out, mix_norm, ff2_norm, ff2_w_in,
            ff2_w_out, ple_norm, ple_w_gate, ple_w_proj, ab_w_in, mla_q_norm, mla_w_uq,
            mla_kv_norm, mla_w_ukv, ab_w_out, fox_w_in, fox_b_f, fox_w_out, final_norm,
            c_ident, c_upper, c_mask, c_cos, c_sin, c_onehot, c_future, out):
    f32, f32r = mybir.dt.float32, mybir.dt.float32r
    ACT = mybir.ActivationFunctionType
    AX = mybir.AxisListType

    ctx = ExitStack()
    with ctx:
        def sb(name, shape, dt=f32):
            return ctx.enter_context(nc.sbuf_tensor(name, shape, dt))

        def sem(name):
            return ctx.enter_context(nc.semaphore(name))

        raw = sb("raw", [P, RING, UNIT])
        w_hi = sb("w_hi", [P, RING, UNIT], f32r)
        w_lo = sb("w_lo", [P, RING, UNIT], f32r)
        x = sb("x", [P, T, D])
        xn = sb("xn", [P, T, D])
        h_hi = sb("h_hi", [P, KD, SEQ], f32r)
        h_lo = sb("h_lo", [P, KD, SEQ], f32r)
        act_a = sb("act_a", [P, 512])
        hid = sb("hid", [P, 512])
        hid_hi = sb("hid_hi", [P, 2, SEQ], f32r)
        hid_lo = sb("hid_lo", [P, 2, SEQ], f32r)
        gain = sb("gain", [P, 2, D])
        meansq = sb("meansq", [P, T])
        minus_half = sb("minus_half", [P, 2 * T])
        rstd = sb("rstd", [P, T])
        pT_hi = sb("pT_hi", [P, LAYERS, 2, SEQ], f32r)
        pT_lo = sb("pT_lo", [P, LAYERS, 2, SEQ], f32r)
        q_tok = sb("q_tok", [P, T, A_HEADS * A_DIM + B_HEADS * QK_B])
        k_tok = sb("k_tok", [P, T, D])
        v_tok = sb("v_tok", [P, T, D])
        comp = sb("comp", [P, T, MLA_C])
        comp_n = sb("comp_n", [P, T, Q_RANK + KV_RANK])
        cT_hi = sb("cT_hi", [P, 3, SEQ], f32r)
        cT_lo = sb("cT_lo", [P, 3, SEQ], f32r)
        c_meansq = sb("c_meansq", [P, T, 2])
        c_rstd = sb("c_rstd", [P, T, 2])
        c_gain = sb("c_gain", [P, Q_RANK + KV_RANK])
        rope_t = sb("rope_t", [P, 4, T, B_HEADS, ROPE // 2])
        stage = sb("stage", [P, 2, 4, QK_B])
        qkT = sb("qkT", [P, 2, 512])
        neg_logits = sb("neg_logits", [P, 2, 384])
        neg_max = sb("neg_max", [P, 2, T])
        probs = sb("probs", [P, 2, 384])
        row_sum = sb("row_sum", [P, 2, T])
        row_inv = sb("row_inv", [P, 2, T])
        probsT = sb("probsT", [P, 2, 384])
        bias = sb("bias", [P, A_HEADS, 384])
        aug_q = sb("aug_q", [P, T, C_HEADS, AUG])
        aug_k = sb("aug_k", [P, T, C_HEADS, AUG])
        forget = sb("forget", [P, 5, T, C_HEADS])
        ident = sb("ident", [P, P])
        upper = sb("upper", [P, 2 * P])
        mask = sb("mask", [P, 384])
        cos = sb("cos", [P, T, ROPE // 2])
        sin = sb("sin", [P, T, ROPE // 2])
        t5_sb = sb("t5_sb", [32, A_HEADS])
        p_sb = k_tok[:, 1, :].rearrange("p (l t c) -> p l t c", l=LAYERS, t=T)
        t5_row, future, onehot = q_tok[0:A_HEADS, 0, 0:512], q_tok[0:A_HEADS, 0, 512:1024], k_tok[0:32, 0, 0:512]
        b_f = sb("b_f", [P, C_HEADS])
        t5_dram = nc.dram_tensor("t5_scratch", [A_HEADS, P, 512], f32, kind="Internal")

        bank = [ctx.enter_context(nc.psum_tensor(f"bank{i}", [P, 512], f32)) for i in range(8)]
        GATE, UP = bank[4], bank[5]

        raw_landed = [sem(f"raw_landed{s}") for s in range(RING)]
        hi_split = sem("hi_split")
        lo_split = sem("lo_split")
        unit_used = sem("unit_used")
        x_landed = sem("x_landed")
        const_landed = sem("const_landed")
        t5_landed = sem("t5_landed")
        gain_landed = [sem("gain_landed0"), sem("gain_landed1")]
        x_ready = sem("x_ready")
        meansq_ready = sem("meansq_ready")
        rstd_ready = sem("rstd_ready")
        root_step = sem("root_step")
        c_rstd_ready = sem("c_rstd_ready")
        xn_ready = sem("xn_ready")
        t_done = sem("t_done")
        h_hi_ready = sem("h_hi_ready")
        h_lo_ready = sem("h_lo_ready")
        y_half = sem("y_half")
        silu_done = sem("silu_done")
        hid_done = sem("hid_done")
        hid_hi_done = sem("hid_hi_done")
        hid_lo_done = sem("hid_lo_done")
        sig_done = sem("sig_done")
        gated = sem("gated")
        pT_done = sem("pT_done")
        pT_hi_done = sem("pT_hi_done")
        pT_lo_done = sem("pT_lo_done")
        t5_done = sem("t5_done")
        t5_row_done = sem("t5_row_done")
        t5_stored = sem("t5_stored")
        mix_act = sem("mix_act")
        mix_dve = sem("mix_dve")
        comp_sq = sem("comp_sq")
        comp_ready = sem("comp_ready")
        cT_done = sem("cT_done")
        cT_hi_done = sem("cT_hi_done")
        cT_lo_done = sem("cT_lo_done")
        rope_step = sem("rope_step")
        f_step = sem("f_step")
        f_act = sem("f_act")
        cum_done = sem("cum_done")
        aug_ready = sem("aug_ready")
        staged = sem("staged")
        qkT_done = sem("qkT_done")
        qkT_copied = sem("qkT_copied")
        logits_done = sem("logits_done")
        biased = sem("biased")
        max_done = sem("max_done")
        exp_done = sem("exp_done")
        probsT_done = sem("probsT_done")
        probsT_copied = sem("probsT_copied")
        inv_done = sem("inv_done")
        pv_done = sem("pv_done")
        head_done = sem("head_done")
        out_stored = sem("out_stored")

        FINAL = 4 * LAYERS
        CONSTS = 12
        F_Z, F_ABS, F_EXP, F_LN, F_LOG = range(5)
        F_STEPS = 3
        Y_HALF = {}
        for layer in range(LAYERS):
            for name in (("ffn", 2 * layer), ("out", layer), ("ffn", 2 * layer + 1), ("gate", layer)):
                Y_HALF[name] = len(Y_HALF) + 1
        norm_gain = []
        for layer in range(LAYERS):
            norm_gain += [ff1_norm[layer:layer + 1, :], mix_norm[layer:layer + 1, :],
                          ff2_norm[layer:layer + 1, :], ple_norm[layer:layer + 1, :]]
        norm_gain.append(final_norm.unsqueeze(0))

        def t_index(b):
            layer, k = divmod(b, 4)
            return 5 * layer + (k if k < 2 else k + 1)

        block = ctx.enter_context(nc.Block())

        @block.sync
        def _(sp):
            def load(n, source, i=0):
                if n >= RING:
                    sp.wait_ge(lo_split, 2 * (n - RING + 1) + 2 * RING * i)
                chunks = source.shape[1]
                sp.dma_start(raw[:, n % RING, 0:WIDTHS[n]].rearrange("p (k c) -> p k c", k=chunks),
                             source).then_inc(raw_landed[n % RING], 16)

            def rows(w, k0, nk, c0, width):
                return w[k0 * P:(k0 + nk) * P, c0:c0 + width].rearrange("(k p) c -> p k c", p=P)

            for b in range(T):
                sp.dma_start(x[:, b, :], x_in[0, b * P:(b + 1) * P, :]).then_inc(x_landed, 16)
            for layer in range(LAYERS):
                for half in range(2):
                    f = 2 * layer + half
                    w_in = (ff1_w_in, ff2_w_in)[half][layer, :, :].rearrange("(k p) c -> p k c", p=P)
                    w_out = (ff1_w_out, ff2_w_out)[half][layer, :, :].rearrange("(g p) c -> p g c", p=P)
                    n = START["ffn", f]

                    def gate_u(i):
                        return w_in[:, :, bass.ds(i * 256, 256)]

                    def up_u(i):
                        return w_in[:, :, bass.ds(i * 256 + FF, 256)]

                    def down_u(i):
                        return w_out[:, bass.ds(i * 2, 2), :]

                    load(n, gate_u(0))
                    load(n + 1, up_u(0))
                    load(n + 2, gate_u(1))
                    load(n + 3, down_u(0))
                    load(n + 4, up_u(1))
                    with sp.Fori(0, PAIRS - 2) as i:
                        load(n + 5, gate_u(i + 2), i)
                        load(n + 6, down_u(i + 1), i)
                        load(n + 7, up_u(i + 2), i)
                    load(n + 32, down_u(PAIRS - 1))
                    if half == 0 and layer == 0:
                        for j in range(4):
                            load(START["ab1"] + j, rows(ab_w_in[0], 2 * j, 2, 0, AB1))
                        for j in range(4):
                            load(START["ab2"] + j, rows(ab_w_in[0], 2 * j, 2, AB1, AB2))
                        load(START["uq"], rows(mla_w_uq[0], 0, 2, 0, B_HEADS * QK_B))
                        load(START["ukv"], rows(mla_w_ukv[0], 0, 1, 0, B_HEADS * (NOPE + VDIM)))
                    if half == 0 and layer == 1:
                        for c, name in enumerate(("fox_q", "fox_k", "fox_v")):
                            for j in range(4):
                                load(START[name] + j, rows(fox_w_in[0], 2 * j, 2, c * D, D))
                        with nc.allow_non_contiguous_dma(reason="sixteen columns of gates"):
                            load(START["fox_f"], rows(fox_w_in[0], 0, KD, 3 * D, C_HEADS))
                    if half == 0:
                        w = (ab_w_out, fox_w_out)[layer][0]
                        for j in range(4):
                            load(START["out", layer] + j, rows(w, 2 * j, 2, 0, D))
                load(START["proj", layer], rows(ple_w_proj[layer], 0, 2, 0, D))
                for j in range(4):
                    load(START["gate", layer] + j, rows(ple_w_gate[layer], 2 * j, 2, 0, D))
            for t in range(T):
                sp.wait_ge(xn_ready, T * FINAL + t + 1)
                sp.dma_start(out[0, t * P:(t + 1) * P, :], xn[:, t, :]).then_inc(out_stored, 16)
            sp.wait_ge(out_stored, 16 * T)

        @block.gpsimd
        def _(pool):
            pool.dma_start(ident[:, :], c_ident).then_inc(const_landed, 16)
            pool.dma_start(gain[:, 0, :], norm_gain[0].partition_broadcast(P)).then_inc(gain_landed[0], 16)
            pool.dma_start(p_sb[:, :, :, :].rearrange("q l t c -> q (l t) c"),
                           p_in.rearrange("l b (t q) c -> q (l b t) c", q=P)).then_inc(const_landed, 16)
            pool.dma_start(gain[:, 1, :], norm_gain[1].partition_broadcast(P)).then_inc(gain_landed[1], 16)
            pool.dma_start(t5_sb[:, :], t5_bias).then_inc(const_landed, 16)
            pool.dma_start(onehot, c_onehot).then_inc(const_landed, 16)
            pool.dma_start(future, c_future).then_inc(const_landed, 16)
            pool.dma_start(upper[:, :], c_upper).then_inc(const_landed, 16)
            pool.dma_start(mask[:, :], c_mask).then_inc(const_landed, 16)
            pool.dma_start(cos[:, :, :], c_cos.rearrange("(t p) c -> p t c", p=P)).then_inc(const_landed, 16)
            pool.dma_start(sin[:, :, :], c_sin.rearrange("(t p) c -> p t c", p=P)).then_inc(const_landed, 16)
            pool.dma_start(c_gain[:, 0:Q_RANK], mla_q_norm.partition_broadcast(P)).then_inc(const_landed, 16)
            pool.dma_start(c_gain[:, Q_RANK:], mla_kv_norm.partition_broadcast(P)).then_inc(const_landed, 16)
            pool.dma_start(b_f[:, :], fox_b_f.partition_broadcast(P)).then_inc(const_landed, 16)
            def load_gain(b):
                pool.wait_ge(xn_ready, T * (b - 1))
                pool.dma_start(gain[:, b % 2, :], norm_gain[b].partition_broadcast(P)).then_inc(
                    gain_landed[b % 2], 16)

            roots = [0]

            def inverse_root(to, mean, exponent):
                nc.gpsimd.tensor_scalar(mean, mean, EPS, None, ALU.add).then_inc(root_step, 1)
                roots[0] += 1
                pool.wait_ge(root_step, roots[0])
                return nc.gpsimd.tensor_tensor(to, mean, exponent, ALU.pow)

            def rstds(b):
                for t in range(T):
                    pool.wait_ge(meansq_ready, T * b + t + 1)
                    inverse_root(rstd[:, t:t + 1], meansq[:, t:t + 1], minus_half[:, 0:1]).then_inc(rstd_ready, 1)

            def stage_head(h, count, kinds, d):
                s = count[0] % 2
                wait_h, hh = count[1], h
                if wait_h is not None:
                    pool.wait_ge(qkT_done, wait_h)
                last = len(kinds) - 1
                for j, (block0, width, at, source) in enumerate(kinds):
                    ins = nc.gpsimd.tensor_copy(stage[:, s, block0:block0 + T, at:at + width], source(hh))
                    if j == last:
                        ins.then_inc(staged, 1)

            def stage_heads(first, heads, kinds, d):
                for h in range(2):
                    stage_head(h, (first + h, first + h - 1 if first + h >= 2 else None), kinds, d)
                with pool.Fori(0, heads // 2 - 1) as i:
                    for s in range(2):
                        stage_head(i * 2 + (2 + s), (first + s, i * 2 + (first + s + 1)), kinds, d)

            nc.gpsimd.memset(stage[:, :, :, :], 0.0).then_inc(root_step, 1)
            roots[0] += 1
            nc.gpsimd.memset(minus_half[:, :], -0.5).then_inc(root_step, 1)
            roots[0] += 1
            pool.wait_ge(t5_row_done, 1)
            pool.dma_start(t5_dram.ap(), t5_row.unsqueeze(1).to_broadcast([A_HEADS, P, 512])).then_inc(t5_stored, 16)
            pool.wait_ge(t5_stored, 16)
            for c0, c1, ahead in ((0, SEQ, 0), (SEQ, 384, P)):
                toeplitz = bass.AP(tensor=t5_dram, offset=P - 1 + ahead,
                                   ap=[[511, P], [P * 512, A_HEADS], [1, c1 - c0]])
                pool.dma_start(bias[:, :, c0:c1], toeplitz).then_inc(t5_landed, 16)
            rstds(0)
            load_gain(2)
            rstds(1)
            load_gain(3)
            half = ROPE // 2
            steps = [0]

            def rope_op(out_, a, b, op):
                nc.gpsimd.tensor_tensor(out_, a, b, op).then_inc(rope_step, 1)
                steps[0] += 1

            def rotate(x1, x2, co, si, tmp):
                rope_op(tmp[0], x1, co, ALU.mult)
                rope_op(tmp[1], x2, si, ALU.mult)
                rope_op(tmp[2], x1, si, ALU.mult)
                rope_op(tmp[3], x2, co, ALU.mult)
                pool.wait_ge(rope_step, steps[0])
                rope_op(x1, tmp[0], tmp[1], ALU.subtract)
                rope_op(x2, tmp[2], tmp[3], ALU.add)

            pool.wait_ge(comp_sq, 4)
            inverse_root(c_rstd[:, :, :].rearrange("p t c -> p (t c)"),
                         c_meansq[:, :, :].rearrange("p t c -> p (t c)"), minus_half[:, :]).then_inc(c_rstd_ready, 1)
            pool.wait_ge(mix_dve, 2)
            pool.wait_ge(const_landed, 16 * CONSTS)
            rotate(comp[:, :, Q_RANK + KV_RANK:Q_RANK + KV_RANK + half],
                   comp[:, :, Q_RANK + KV_RANK + half:MLA_C], cos[:, :, :], sin[:, :, :],
                   [rope_t[:, j, :, 0, :] for j in range(4)])
            pool.wait_ge(mix_act, 1)
            stage_heads(0, A_HEADS, [
                (0, A_DIM, 0, lambda h: q_tok[:, :, bass.ds(h * A_DIM, A_DIM)]),
                (2, A_DIM, 0, lambda h: k_tok[:, :, bass.ds(h * A_DIM, A_DIM)])], A_DIM)
            pool.wait_ge(mix_act, 4)
            pool.wait_ge(mix_dve, 4)
            q_b = q_tok[:, :, A_HEADS * A_DIM:].rearrange("p t (h c) -> p t h c", h=B_HEADS)
            for t in range(T):
                wide = [P, B_HEADS, half]
                rotate(q_b[:, t, :, NOPE:NOPE + half], q_b[:, t, :, NOPE + half:QK_B],
                       cos[:, t:t + 1, :].to_broadcast(wide), sin[:, t:t + 1, :].to_broadcast(wide),
                       [rope_t[:, j, t, :, :] for j in range(4)])
            pool.wait_ge(rope_step, steps[0])
            stage_heads(A_HEADS, B_HEADS, [
                (0, QK_B, 0, lambda h: q_tok[:, :, bass.ds(h * QK_B + A_HEADS * A_DIM, QK_B)]),
                (2, NOPE, 0, lambda h: k_tok[:, :, bass.ds(h * NOPE + A_HEADS * A_DIM, NOPE)]),
                (2, ROPE, NOPE, lambda h: comp[:, :, Q_RANK + KV_RANK:MLA_C])], QK_B)
            for b in range(2, 6):
                rstds(b)
                load_gain(b + 2)
            pool.wait_ge(aug_ready, 1)
            pool.wait_ge(mix_act, 6)
            stage_heads(HEADS, C_HEADS, [
                (0, C_DIM, 0, lambda h: q_tok[:, :, bass.ds(h * C_DIM, C_DIM)]),
                (2, C_DIM, 0, lambda h: k_tok[:, :, bass.ds(h * C_DIM, C_DIM)]),
                (0, AUG, C_DIM, lambda h: aug_q[:, :, bass.ds(h, 1), :].rearrange("p t h c -> p t (h c)")),
                (2, AUG, C_DIM, lambda h: aug_k[:, :, bass.ds(h, 1), :].rearrange("p t h c -> p t (h c)"))],
                C_DIM + AUG)
            for b in range(6, FINAL + 1):
                rstds(b)
                if b + 2 <= FINAL:
                    load_gain(b + 2)

        @block.tensor
        def _(pe):
            Y = [[bank[0], bank[1]], [bank[2], bank[3]]]
            Z = [[bank[4], bank[5]], [bank[6], bank[7]]]

            def product(out_, a_hi, a_lo, b_hi, b_lo, start, stop):
                nc.tensor.matmul(out_, a_hi, b_hi, start=start, stop=False)
                nc.tensor.matmul(out_, a_hi, b_lo, start=False, stop=False)
                return nc.tensor.matmul(out_, a_lo, b_hi, start=False, stop=stop)

            def wide_unit(n, hi, lo, k0, banks, first, last, i=0, tokens_outer=False):
                chunks = 1 if n == START["ukv"] else 2
                width = WIDTHS[n] // chunks
                s = n % RING
                pe.wait_ge(lo_split, i * (2 * RING) + 2 * (n + 1))
                if tokens_outer:
                    order = [(t, k) for t in range(T) for k in range(chunks)]
                else:
                    order = [(t, k) for k in range(chunks) for t in range(T)]
                for t, k in order:
                    for c in range((width + 511) // 512):
                        c0, c1 = k * width + 512 * c, k * width + min(512 * (c + 1), width)
                        ins = product(banks[t][c][:, 0:c1 - c0],
                                      hi[:, k0 + k, t * P:(t + 1) * P], lo[:, k0 + k, t * P:(t + 1) * P],
                                      w_hi[:, s, c0:c1], w_lo[:, s, c0:c1],
                                      start=first and k == 0, stop=last and k == chunks - 1)
                    if tokens_outer and (t, k) == (0, chunks - 1):
                        ins.then_inc(y_half, 1)
                ins.then_inc(unit_used, 1)

            def narrow_unit(n, target, i=0):
                s = n % RING
                hi = w_hi[:, s, :].rearrange("p (k c) -> p k c", k=KD)
                lo = w_lo[:, s, :].rearrange("p (k c) -> p k c", k=KD)
                for g in range(2):
                    for k in range(KD):
                        if g == 0 and k == 0:
                            pe.wait_ge(lo_split, i * (2 * RING) + (2 * n + 1))
                        if g == 0 and k == KD // 2:
                            pe.wait_ge(lo_split, i * (2 * RING) + (2 * n + 2))
                        dst = target[:, g * SEQ:(g + 1) * SEQ]
                        w = slice(g * P, (g + 1) * P)
                        ins = product(dst, hi[:, k, w], lo[:, k, w], h_hi[:, k, :], h_lo[:, k, :],
                                      start=k == 0, stop=k == KD - 1)
                ins.then_inc(unit_used, 1)

            def transpose_input(r, source, ready, at):
                for t in range(T):
                    pe.wait_ge(ready, at[t])
                    for k in range(KD):
                        ins = nc.tensor.transpose(bank[2 * t + k // 4][:, (k % 4) * P:(k % 4 + 1) * P],
                                                  source[:, t, k * P:(k + 1) * P], ident[:, :])
                        if k % 4 == 3:
                            ins.then_inc(t_done, 1)
                pe.wait_ge(h_hi_ready, 4 * r + 4)
                pe.wait_ge(h_lo_ready, 4 * r + 4)

            def normed_input(b):
                transpose_input(t_index(b), xn, xn_ready, [T * b + 1, T * b + 2])

            def ffn(f):
                n, p0 = START["ffn", f], PAIRS * f

                def gate(n, pair, i=0):
                    if n > FFN_UNITS or n > 0 and pair > 0:
                        pe.wait_ge(silu_done, i + pair)
                    narrow_unit(n, GATE, i)

                def up(n, pair, i=0):
                    if pair > 0:
                        pe.wait_ge(hid_done, i + pair)
                    narrow_unit(n, UP, i)

                def down(n, pair, i=0, first=False, last=False):
                    pe.wait_ge(hid_lo_done, i + (pair + 1))
                    wide_unit(n, hid_hi, hid_lo, 0, Y, first, last, i, tokens_outer=last)

                gate(n, p0)
                up(n + 1, p0)
                gate(n + 2, p0 + 1)
                down(n + 3, p0, first=True)
                up(n + 4, p0 + 1)
                with pe.Fori(0, PAIRS - 2) as i:
                    gate(n + 5, p0 + 2, i)
                    down(n + 6, p0 + 1, i)
                    up(n + 7, p0 + 2, i)
                down(n + 32, p0 + PAIRS - 1, last=True)

            def project(name, hi, lo, banks, tokens_outer=False):
                for j in range(4):
                    wide_unit(START[name] + j, hi, lo, 2 * j, banks, j == 0, j == 3,
                              tokens_outer=tokens_outer and j == 3)

            def attend(first, heads, d, dt):
                def logits(h, s, i=None):
                    at = (lambda v: v) if i is None else (lambda v: i * 2 + v)
                    qk, lg = bank[2 + s], bank[4 + s]
                    pe.wait_ge(staged, at(h + 1))
                    if h >= 2:
                        pe.wait_ge(qkT_copied, at(h - 1))
                    for j in range(4):
                        ins = nc.tensor.transpose(qk[0:dt, j * P:(j + 1) * P], stage[:, s, j, 0:dt], ident[:, :])
                    ins.then_inc(qkT_done, 1)
                    pe.wait_ge(qkT_copied, at(h + 1))
                    if h >= 2:
                        pe.wait_ge(max_done, at(h - 1))
                    nc.tensor.matmul(lg[:, 0:SEQ], qkT[0:d, s, P:2 * P], qkT[0:d, s, 2 * P:4 * P],
                                     start=True, stop=True)
                    nc.tensor.matmul(lg[:, SEQ:SEQ + P], qkT[0:d, s, 0:P], qkT[0:d, s, 2 * P:3 * P],
                                     start=True, stop=True).then_inc(logits_done, 1)

                def values(h, s, i=None):
                    at = (lambda v: v) if i is None else (lambda v: i * 2 + v)
                    pT, o = bank[6 + s], bank[s]
                    pe.wait_ge(exp_done, at(h + 1))
                    if h >= 2:
                        pe.wait_ge(probsT_copied, at(h - 1))
                    for j in range(3):
                        ins = nc.tensor.transpose(pT[:, j * P:(j + 1) * P], probs[:, s, j * P:(j + 1) * P],
                                                  ident[:, :])
                    ins.then_inc(probsT_done, 1)
                    pe.wait_ge(probsT_copied, at(h + 1))
                    if h >= 2:
                        pe.wait_ge(head_done, at(h - 1))
                    col = h % HEADS * 64 if i is None else i * 128 + h % HEADS * 64
                    v = [v_tok[:, t, bass.ds(col, 64)] for t in range(T)]
                    nc.tensor.matmul(o[:, 0:64], probsT[:, s, 2 * P:3 * P], v[0], start=True, stop=True)
                    nc.tensor.matmul(o[:, 64:128], probsT[:, s, 0:P], v[0], start=True, stop=False)
                    nc.tensor.matmul(o[:, 64:128], probsT[:, s, P:2 * P], v[1], start=False,
                                     stop=True).then_inc(pv_done, 1)

                logits(first, 0)
                logits(first + 1, 1)
                with pe.Fori(0, heads // 2 - 1) as i:
                    for s in range(2):
                        values(first + s, s, i)
                        logits(first + 2 + s, s, i)
                for s in range(2):
                    values(first + heads - 2 + s, s)

            pe.wait_ge(const_landed, 16 * CONSTS)
            for layer in range(LAYERS):
                for k in range(2):
                    for t in range(T):
                        ins = nc.tensor.transpose(bank[4 + layer][:, k * SEQ + t * P:k * SEQ + (t + 1) * P],
                                                  p_sb[:, layer, t, k * P:(k + 1) * P], ident[:, :])
                ins.then_inc(pT_done, 1)
            nc.tensor.matmul(bank[6][0:A_HEADS, :], t5_sb[:, :], onehot, start=True,
                             stop=True).then_inc(t5_done, 1)
            for layer in range(LAYERS):
                b = 4 * layer
                normed_input(b)
                if layer == 0:
                    pe.wait_ge(pT_lo_done, 2)
                ffn(2 * layer)
                normed_input(b + 1)
                if layer == 0:
                    project("ab1", h_hi, h_lo, Y)
                    pe.wait_ge(t5_row_done, 1)
                    project("ab2", h_hi, h_lo, Z)
                    pe.wait_ge(mix_act, 1)
                    pe.wait_ge(mix_dve, 1)
                    for t in range(T):
                        pe.wait_ge(comp_ready, t + 1)
                        for k in range(3):
                            ins = nc.tensor.transpose(bank[t][:, k * P:(k + 1) * P],
                                                      comp_n[:, t, k * P:(k + 1) * P], ident[:, :])
                        ins.then_inc(cT_done, 1)
                    pe.wait_ge(cT_lo_done, 2)
                    pe.wait_ge(mix_act, 2)
                    wide_unit(START["uq"], cT_hi, cT_lo, 0, Z, True, True)
                    wide_unit(START["ukv"], cT_hi, cT_lo, 2, Y, True, True)
                    pe.wait_ge(mix_act, 4)
                    pe.wait_ge(mix_dve, 4)
                    attend(0, A_HEADS, A_DIM, QK_B)
                    attend(A_HEADS, B_HEADS, QK_B, QK_B)
                else:
                    project("fox_q", h_hi, h_lo, Y)
                    project("fox_k", h_hi, h_lo, Z)
                    pe.wait_ge(mix_act, 5)
                    pe.wait_ge(mix_dve, 5)
                    project("fox_v", h_hi, h_lo, Y)
                    pe.wait_ge(mix_dve, 6)
                    pe.wait_ge(mix_act, 6)
                    n = START["fox_f"]
                    pe.wait_ge(lo_split, 2 * (n + 1))
                    for t in range(T):
                        for k in range(KD):
                            cols = slice(k * C_HEADS, (k + 1) * C_HEADS)
                            ins = product(bank[4][:, t * C_HEADS:(t + 1) * C_HEADS],
                                          h_hi[:, k, t * P:(t + 1) * P], h_lo[:, k, t * P:(t + 1) * P],
                                          w_hi[:, n % RING, cols], w_lo[:, n % RING, cols],
                                          start=k == 0, stop=k == KD - 1)
                    ins.then_inc(unit_used, 1)
                    pe.wait_ge(f_step, F_STEPS)
                    lf = forget[:, F_LOG, :, :]
                    nc.tensor.matmul(bank[5][:, 0:C_HEADS], upper[:, P:2 * P], lf[:, 0, :], start=True, stop=True)
                    nc.tensor.matmul(bank[5][:, C_HEADS:2 * C_HEADS], upper[:, 0:P], lf[:, 0, :], start=True,
                                     stop=False)
                    nc.tensor.matmul(bank[5][:, C_HEADS:2 * C_HEADS], upper[:, P:2 * P], lf[:, 1, :],
                                     start=False, stop=True).then_inc(cum_done, 1)
                    pe.wait_ge(mix_act, 7)
                    pe.wait_ge(mix_dve, 7)
                    pe.wait_ge(aug_ready, 1)
                    attend(HEADS, C_HEADS, C_DIM + AUG, C_DIM + AUG)
                heads_done = HEADS * (layer + 1)
                transpose_input(5 * layer + 2, xn, head_done, [heads_done, heads_done])
                project(("out", layer), h_hi, h_lo, Y, tokens_outer=True)
                normed_input(b + 2)
                ffn(2 * layer + 1)
                wide_unit(START["proj", layer], pT_hi[:, layer, :, :], pT_lo[:, layer, :, :], 0, Z, True, True)
                normed_input(b + 3)
                project(("gate", layer), h_hi, h_lo, Y, tokens_outer=True)

        @block.scalar
        def _(act):
            def split(n, i=0):
                if n >= N_UNITS:
                    return
                s, half = n % RING, WIDTHS[n] // 2
                act.wait_ge(raw_landed[s], 16 * (n // RING + 1) + i * 16)
                if n >= RING:
                    act.wait_ge(unit_used, i * RING + (n - RING + 1))
                for j in range(2):
                    cols = slice(j * half, (j + 1) * half)
                    nc.scalar.copy(w_hi[:, s, cols], raw[:, s, cols]).then_inc(hi_split, 1)

            def splits_behind(name, count):
                for j in range(count):
                    split(START[name] + j + RING - 1)

            def mean_squares(b):
                for t in range(T):
                    if b == 0:
                        act.wait_ge(x_landed, 16 * T)
                    else:
                        act.wait_ge(x_ready, T * (b - 1) + t + 1)
                    nc.scalar.activation(xn[:, t, :], x[:, t, :], ACT.Square, scale=D ** -0.5,
                                         accum_out=meansq[:, t:t + 1]).then_inc(meansq_ready, 1)

            def input_hi(r):
                for j in range(4):
                    act.wait_ge(t_done, 4 * r + j + 1)
                    nc.scalar.copy(h_hi[:, 4 * (j % 2):4 * (j % 2) + 4, (j // 2) * P:(j // 2 + 1) * P],
                                   bank[j][:, :].rearrange("p (k c) -> p k c", k=4)).then_inc(h_hi_ready, 1)

            def normed_input(b):
                mean_squares(b)
                input_hi(t_index(b))

            def ffn(f):
                n, p0 = START["ffn", f], PAIRS * f

                def silu(n, i=0):
                    act.wait_ge(unit_used, i * RING + (n + 1))
                    nc.scalar.activation(act_a[:, :], GATE[:, :], ACT.Silu).then_inc(silu_done, 1)

                def hidden_hi(pair, i=0):
                    act.wait_ge(hid_done, i + (pair + 1))
                    nc.scalar.copy(hid_hi[:, :, :], hid[:, :].rearrange("p (g c) -> p g c", g=2)).then_inc(
                        hid_hi_done, 1)

                split(n + 2)
                silu(n)
                split(n + 3)
                hidden_hi(p0)
                split(n + 4)
                silu(n + 2)
                split(n + 5)
                split(n + 6)
                hidden_hi(p0 + 1)
                with act.Fori(0, PAIRS - 2) as i:
                    split(n + 7, i)
                    silu(n + 5, i)
                    split(n + 8, i)
                    split(n + 9, i)
                    hidden_hi(p0 + 2, i)
                split(n + 34)

            def attend(first, heads, d):
                def copy_qkT(h, s, at):
                    act.wait_ge(qkT_done, at(h + 1))
                    if h >= 2:
                        act.wait_ge(logits_done, at(h - 1))
                    nc.scalar.copy(qkT[0:d, s, :], bank[2 + s][0:d, :]).then_inc(qkT_copied, 1)

                def exps(h, s, at):
                    act.wait_ge(max_done, at(h + 1))
                    if h >= 2:
                        act.wait_ge(probsT_done, at(h - 1))
                        act.wait_ge(inv_done, at(h - 1))
                    nc.scalar.activation(probs[:, s, 0:SEQ], neg_logits[:, s, 0:SEQ], ACT.Exp, scale=-1.0,
                                         bias=neg_max[:, s, 1:2], accum_out=row_sum[:, s, 1:2])
                    nc.scalar.activation(probs[:, s, SEQ:], neg_logits[:, s, SEQ:], ACT.Exp, scale=-1.0,
                                         bias=neg_max[:, s, 0:1], accum_out=row_sum[:, s, 0:1]).then_inc(exp_done, 1)

                for s in range(2):
                    copy_qkT(first + s, s, lambda v: v)
                with act.Fori(0, heads // 2 - 1) as i:
                    for s in range(2):
                        exps(first + s, s, lambda v: i * 2 + v)
                        copy_qkT(first + 2 + s, s, lambda v: i * 2 + v)
                for s in range(2):
                    exps(first + heads - 2 + s, s, lambda v: v)

            for n in range(RING - 1):
                split(n)
            for layer in range(LAYERS):
                act.wait_ge(pT_done, layer + 1)
                nc.scalar.copy(pT_hi[:, layer, :, :],
                               bank[4 + layer][:, :].rearrange("p (k c) -> p k c", k=2)).then_inc(pT_hi_done, 1)
            for layer in range(LAYERS):
                b = 4 * layer
                normed_input(b)
                ffn(2 * layer)
                normed_input(b + 1)
                if layer == 0:
                    splits_behind("ab1", 4)
                    act.wait_ge(unit_used, START["ab1"] + 4)
                    act.wait_ge(t5_stored, 16)
                    for t in range(T):
                        ins = nc.scalar.mul(q_tok[:, t, 0:512], bank[2 * t][:, :], -A_DIM ** -0.5)
                    ins.then_inc(mix_act, 1)
                    splits_behind("ab2", 3)
                    act.wait_ge(unit_used, START["ab2"] + 4)
                    for t in range(T):
                        ins = nc.scalar.copy(v_tok[:, t, 0:512], bank[4 + 2 * t][:, :])
                    ins.then_inc(mix_act, 1)
                    act.wait_ge(mix_dve, 2)
                    for t in range(T):
                        for j, (c0, c1) in enumerate(((0, Q_RANK), (Q_RANK, Q_RANK + KV_RANK))):
                            ins = nc.scalar.activation(comp_n[:, t, c0:c1], comp[:, t, c0:c1], ACT.Square,
                                                       scale=(c1 - c0) ** -0.5,
                                                       accum_out=c_meansq[:, t, j:j + 1])
                            ins.then_inc(comp_sq, 1)
                    split(START["ab2"] + 3 + RING - 1)
                    for t in range(T):
                        act.wait_ge(cT_done, t + 1)
                        nc.scalar.copy(cT_hi[:, :, t * P:(t + 1) * P],
                                       bank[t][:, 0:3 * P].rearrange("p (k c) -> p k c", k=3)).then_inc(
                                           cT_hi_done, 1)
                    splits_behind("uq", 1)
                    act.wait_ge(unit_used, START["uq"] + 1)
                    for t in range(T):
                        ins = nc.scalar.mul(q_tok[:, t, 512:1024], bank[4 + 2 * t][:, :], -QK_B ** -0.5)
                    ins.then_inc(mix_act, 1)
                    act.wait_ge(unit_used, START["ukv"] + 1)
                    for t in range(T):
                        kv = bank[2 * t][:, :].rearrange("p (h c) -> p h c", h=4)
                        nc.scalar.copy(k_tok[:, t, 512:768].rearrange("p (h c) -> p h c", h=4), kv[:, :, 0:NOPE])
                        ins = nc.scalar.copy(v_tok[:, t, 512:768].rearrange("p (h c) -> p h c", h=4),
                                             kv[:, :, NOPE:])
                    ins.then_inc(mix_act, 1)
                    splits_behind("ukv", 1)
                    attend(0, A_HEADS, QK_B)
                    attend(A_HEADS, B_HEADS, QK_B)
                else:
                    splits_behind("fox_q", 4)
                    act.wait_ge(unit_used, START["fox_q"] + 4)
                    for t in range(T):
                        ins = nc.scalar.mul(q_tok[:, t, 0:512], bank[2 * t][:, :], -C_DIM ** -0.5)
                    ins.then_inc(mix_act, 1)
                    splits_behind("fox_k", 4)
                    act.wait_ge(unit_used, START["fox_k"] + 4)
                    for t in range(T):
                        ins = nc.scalar.copy(k_tok[:, t, 0:512], bank[4 + 2 * t][:, :])
                    ins.then_inc(mix_act, 1)
                    splits_behind("fox_v", 4)
                    act.wait_ge(unit_used, START["fox_v"] + 4)
                    for t in range(T):
                        ins = nc.scalar.copy(v_tok[:, t, 0:512], bank[2 * t][:, :])
                    ins.then_inc(mix_act, 1)
                    splits_behind("fox_f", 1)
                    act.wait_ge(f_step, 2)
                    nc.scalar.activation(forget[:, F_EXP, :, :], forget[:, F_ABS, :, :], ACT.Exp,
                                         scale=-1.0).then_inc(f_act, 1)
                    act.wait_ge(f_act, 1)
                    nc.scalar.activation(forget[:, F_LN, :, :], forget[:, F_EXP, :, :], ACT.Ln,
                                         bias=1.0).then_inc(f_act, 1)
                    attend(HEADS, C_HEADS, C_DIM + AUG)
                input_hi(5 * layer + 2)
                splits_behind(("out", layer), 4)
                normed_input(b + 2)
                ffn(2 * layer + 1)
                mean_squares(b + 3)
                splits_behind(("proj", layer), 1)
                input_hi(t_index(b + 3))
                splits_behind(("gate", layer), 4)
                for t in range(T):
                    if t == 0:
                        act.wait_ge(y_half, Y_HALF["gate", layer])
                    else:
                        act.wait_ge(unit_used, START["gate", layer] + 4)
                    for c in range(2):
                        nc.scalar.activation(xn[:, t, 512 * c:512 * (c + 1)], bank[2 * t + c][:, :],
                                             ACT.Sigmoid).then_inc(sig_done, 1)
            mean_squares(FINAL)

        @block.vector
        def _(dve):
            def split(n, i=0):
                if n >= N_UNITS:
                    return
                s, half = n % RING, WIDTHS[n] // 2
                for j in range(2):
                    dve.wait_ge(hi_split, i * (2 * RING) + (2 * n + j + 1))
                    cols = slice(j * half, (j + 1) * half)
                    nc.vector.tensor_tensor(w_lo[:, s, cols], raw[:, s, cols], w_hi[:, s, cols].bitcast(f32),
                                            ALU.subtract).then_inc(lo_split, 1)

            def splits_behind(name, count):
                for j in range(count):
                    split(START[name] + j + RING - 1)

            def normalize(b):
                dve.wait_ge(gain_landed[b % 2], 16 * (b // 2 + 1))
                for t in range(T):
                    one = slice(t, t + 1)
                    dve.wait_ge(rstd_ready, T * b + t + 1)
                    nc.vector.scalar_tensor_tensor(xn[:, t, :], x[:, t, :], rstd[:, one], gain[:, b % 2, :],
                                                   ALU.mult, ALU.mult).then_inc(xn_ready, 1)

            def input_lo(r):
                for j in range(4):
                    dve.wait_ge(h_hi_ready, 4 * r + j + 1)
                    rows = slice(4 * (j % 2), 4 * (j % 2) + 4)
                    cols = slice((j // 2) * P, (j // 2 + 1) * P)
                    nc.vector.tensor_tensor(h_lo[:, rows, cols],
                                            bank[j][:, :].rearrange("p (k c) -> p k c", k=4),
                                            h_hi[:, rows, cols].bitcast(f32), ALU.subtract).then_inc(h_lo_ready, 1)

            def residual(name, last_unit, factor):
                for t in range(T):
                    if t == 0:
                        dve.wait_ge(y_half, Y_HALF[name])
                    else:
                        dve.wait_ge(unit_used, last_unit + 1)
                    for c in range(2):
                        cols = slice(512 * c, 512 * (c + 1))
                        ins = nc.vector.scalar_tensor_tensor(x[:, t, cols], bank[2 * t + c][:, :], factor,
                                                             x[:, t, cols], ALU.mult, ALU.add)
                    ins.then_inc(x_ready, 1)

            def ffn(f):
                n, p0 = START["ffn", f], PAIRS * f

                def hidden(n, pair, i=0):
                    dve.wait_ge(silu_done, i + (pair + 1))
                    dve.wait_ge(unit_used, i * RING + (n + 1))
                    nc.vector.tensor_tensor(hid[:, :], act_a[:, :], UP[:, :], ALU.mult).then_inc(hid_done, 1)
                    dve.wait_ge(hid_hi_done, i + (pair + 1))
                    nc.vector.tensor_tensor(hid_lo[:, :, :], hid[:, :].rearrange("p (g c) -> p g c", g=2),
                                            hid_hi[:, :, :].bitcast(f32), ALU.subtract).then_inc(hid_lo_done, 1)

                split(n + 2)
                split(n + 3)
                hidden(n + 1, p0)
                split(n + 4)
                split(n + 5)
                split(n + 6)
                hidden(n + 4, p0 + 1)
                with dve.Fori(0, PAIRS - 2) as i:
                    split(n + 7, i)
                    split(n + 8, i)
                    split(n + 9, i)
                    hidden(n + 7, p0 + 2, i)
                split(n + 34)
                residual(("ffn", f), n + 32, 0.5)

            def attend(first, heads, negated_bias):
                def maxima(h, s, at, head):
                    dve.wait_ge(logits_done, at(h + 1))
                    if h >= 2:
                        dve.wait_ge(exp_done, at(h - 1))
                    nc.vector.tensor_tensor(neg_logits[:, s, :], negated_bias(head), bank[4 + s][:, 0:384],
                                            ALU.add).then_inc(biased, 1)
                    dve.wait_ge(biased, at(h + 1))
                    nc.vector.tensor_reduce(neg_max[:, s, 1:2], neg_logits[:, s, 0:SEQ], AX.X, ALU.min)
                    nc.vector.tensor_reduce(neg_max[:, s, 0:1], neg_logits[:, s, SEQ:], AX.X,
                                            ALU.min).then_inc(max_done, 1)

                def copy_probsT(h, s, at):
                    dve.wait_ge(exp_done, at(h + 1))
                    nc.vector.reciprocal(row_inv[:, s, :], row_sum[:, s, :]).then_inc(inv_done, 1)
                    dve.wait_ge(probsT_done, at(h + 1))
                    if h >= 2:
                        dve.wait_ge(pv_done, at(h - 1))
                    nc.vector.tensor_copy(probsT[:, s, :], bank[6 + s][:, 0:384]).then_inc(probsT_copied, 1)

                def output(h, s, at, column):
                    dve.wait_ge(pv_done, at(h + 1))
                    dve.wait_ge(inv_done, at(h + 1))
                    nc.vector.tensor_tensor(xn[:, :, bass.ds(column, 64)],
                                            bank[s][:, 0:P].rearrange("p (t c) -> p t c", t=T),
                                            row_inv[:, s, :].unsqueeze(2).to_broadcast([P, T, 64]),
                                            ALU.mult).then_inc(head_done, 1)

                f0 = first % HEADS
                for s in range(2):
                    maxima(first + s, s, lambda v: v, s)
                with dve.Fori(0, heads // 2 - 1) as i:
                    for s in range(2):
                        at = lambda v: i * 2 + v
                        copy_probsT(first + s, s, at)
                        maxima(first + 2 + s, s, at, i * 2 + (2 + s))
                        output(first + s, s, at, i * 128 + (f0 + s) * 64)
                for s in range(2):
                    copy_probsT(first + heads - 2 + s, s, lambda v: v)
                    output(first + heads - 2 + s, s, lambda v: v, (f0 + heads - 2 + s) * 64)

            for n in range(RING - 1):
                split(n)
            for layer in range(LAYERS):
                dve.wait_ge(pT_hi_done, layer + 1)
                nc.vector.tensor_tensor(pT_lo[:, layer, :, :],
                                        bank[4 + layer][:, :].rearrange("p (k c) -> p k c", k=2),
                                        pT_hi[:, layer, :, :].bitcast(f32), ALU.subtract).then_inc(pT_lo_done, 1)
            dve.wait_ge(t5_done, 1)
            dve.wait_ge(const_landed, 16 * CONSTS)
            nc.vector.tensor_tensor(t5_row, future, bank[6][0:A_HEADS, :], ALU.add).then_inc(
                t5_row_done, 1)
            for layer in range(LAYERS):
                b = 4 * layer
                normalize(b)
                input_lo(t_index(b))
                ffn(2 * layer)
                normalize(b + 1)
                input_lo(t_index(b + 1))
                if layer == 0:
                    splits_behind("ab1", 4)
                    dve.wait_ge(unit_used, START["ab1"] + 4)
                    for t in range(T):
                        ins = nc.vector.tensor_copy(k_tok[:, t, 0:512], bank[2 * t + 1][:, :])
                    ins.then_inc(mix_dve, 1)
                    splits_behind("ab2", 3)
                    dve.wait_ge(unit_used, START["ab2"] + 4)
                    for t in range(T):
                        ins = nc.vector.tensor_copy(comp[:, t, :], bank[5 + 2 * t][:, 0:MLA_C])
                    ins.then_inc(mix_dve, 1)
                    dve.wait_ge(c_rstd_ready, 1)
                    for t in range(T):
                        for j, (c0, c1) in enumerate(((0, Q_RANK), (Q_RANK, Q_RANK + KV_RANK))):
                            ins = nc.vector.scalar_tensor_tensor(comp_n[:, t, c0:c1], comp[:, t, c0:c1],
                                                                 c_rstd[:, t, j:j + 1], c_gain[:, c0:c1],
                                                                 ALU.mult, ALU.mult)
                        ins.then_inc(comp_ready, 1)
                    split(START["ab2"] + 3 + RING - 1)
                    for t in range(T):
                        dve.wait_ge(cT_hi_done, t + 1)
                        nc.vector.tensor_tensor(cT_lo[:, :, t * P:(t + 1) * P],
                                                bank[t][:, 0:3 * P].rearrange("p (k c) -> p k c", k=3),
                                                cT_hi[:, :, t * P:(t + 1) * P].bitcast(f32),
                                                ALU.subtract).then_inc(cT_lo_done, 1)
                    splits_behind("uq", 1)
                    dve.wait_ge(unit_used, START["uq"] + 1)
                    for t in range(T):
                        ins = nc.vector.tensor_scalar(q_tok[:, t, 1024:1280], bank[5 + 2 * t][:, 0:256],
                                                      -QK_B ** -0.5, None, ALU.mult)
                    ins.then_inc(mix_dve, 1)
                    dve.wait_ge(unit_used, START["ukv"] + 1)
                    for t in range(T):
                        kv = bank[2 * t + 1][:, :].rearrange("p (h c) -> p h c", h=4)
                        nc.vector.tensor_copy(k_tok[:, t, 768:1024].rearrange("p (h c) -> p h c", h=4),
                                              kv[:, :, 0:NOPE])
                        ins = nc.vector.tensor_copy(v_tok[:, t, 768:1024].rearrange("p (h c) -> p h c", h=4),
                                                    kv[:, :, NOPE:])
                    ins.then_inc(mix_dve, 1)
                    splits_behind("ukv", 1)
                    dve.wait_ge(t5_landed, 32)
                    attend(0, A_HEADS, lambda h: bias[:, bass.ds(h, 1), :].rearrange("p h c -> p (h c)"))
                    attend(A_HEADS, B_HEADS, lambda h: mask[:, :])
                else:
                    splits_behind("fox_q", 4)
                    dve.wait_ge(unit_used, START["fox_q"] + 4)
                    for t in range(T):
                        ins = nc.vector.tensor_scalar(q_tok[:, t, 512:1024], bank[2 * t + 1][:, :],
                                                      -C_DIM ** -0.5, None, ALU.mult)
                    ins.then_inc(mix_dve, 1)
                    splits_behind("fox_k", 4)
                    dve.wait_ge(unit_used, START["fox_k"] + 4)
                    for t in range(T):
                        ins = nc.vector.tensor_copy(k_tok[:, t, 512:1024], bank[5 + 2 * t][:, :])
                    ins.then_inc(mix_dve, 1)
                    splits_behind("fox_v", 4)
                    dve.wait_ge(unit_used, START["fox_v"] + 4)
                    for t in range(T):
                        ins = nc.vector.tensor_copy(v_tok[:, t, 512:1024], bank[2 * t + 1][:, :])
                    ins.then_inc(mix_dve, 1)
                    fsteps = [0]

                    def f_next(ins):
                        ins.then_inc(f_step, 1)
                        fsteps[0] += 1
                        dve.wait_ge(f_step, fsteps[0])

                    dve.wait_ge(unit_used, START["fox_f"] + 1)
                    z = forget[:, F_Z, :, :]
                    f_next(nc.vector.tensor_tensor(z, bank[4][:, 0:T * C_HEADS].rearrange("p (t h) -> p t h", t=T),
                                                   b_f[:, :].unsqueeze(1).to_broadcast([P, T, C_HEADS]), ALU.add))
                    f_next(nc.vector.scalar_tensor_tensor(forget[:, F_ABS, :, :], z, -1.0, z, ALU.mult, ALU.max))
                    splits_behind("fox_f", 1)
                    dve.wait_ge(f_act, 2)
                    f_next(nc.vector.scalar_tensor_tensor(forget[:, F_LOG, :, :], z, 0.0, forget[:, F_LN, :, :],
                                                          ALU.min, ALU.subtract))
                    dve.wait_ge(cum_done, 1)
                    cum = bank[5][:, 0:T * C_HEADS].rearrange("p (t h) -> p t h", t=T)
                    nc.vector.memset(aug_q[:, :, :, 0], -1.0)
                    nc.vector.memset(aug_k[:, :, :, 1], 1.0)
                    nc.vector.tensor_scalar(aug_q[:, :, :, 1], cum, -1.0, None, ALU.mult)
                    nc.vector.tensor_scalar(aug_k[:, :, :, 0], cum, -1.0, None, ALU.mult).then_inc(aug_ready, 1)
                    attend(HEADS, C_HEADS, lambda h: mask[:, :])
                input_lo(5 * layer + 2)
                splits_behind(("out", layer), 4)
                residual(("out", layer), START["out", layer] + 3, 1.0)
                normalize(b + 2)
                input_lo(t_index(b + 2))
                ffn(2 * layer + 1)
                normalize(b + 3)
                splits_behind(("proj", layer), 1)
                input_lo(t_index(b + 3))
                splits_behind(("gate", layer), 4)
                for t in range(T):
                    for c in range(2):
                        cols = slice(512 * c, 512 * (c + 1))
                        tile = 2 * t + c
                        dve.wait_ge(sig_done, 4 * layer + tile + 1)
                        nc.vector.tensor_tensor(xn[:, t, cols], xn[:, t, cols], bank[4 + tile][:, :],
                                                ALU.mult).then_inc(gated, 1)
                        dve.wait_ge(gated, 4 * layer + tile + 1)
                        ins = nc.vector.tensor_tensor(x[:, t, cols], x[:, t, cols], xn[:, t, cols], ALU.add)
                    ins.then_inc(x_ready, 1)
            normalize(FINAL)


_INS = ["x", "p", "t5_bias", "ff1_norm", "ff1_w_in", "ff1_w_out", "mix_norm", "ff2_norm", "ff2_w_in",
        "ff2_w_out", "ple_norm", "ple_w_gate", "ple_w_proj", "ab_w_in", "mla_q_norm", "mla_w_uq",
        "mla_kv_norm", "mla_w_ukv", "ab_w_out", "fox_w_in", "fox_b_f", "fox_w_out", "final_norm"]


def constants():
    import math
    import numpy as np
    f = np.float32
    token = np.arange(P)
    upper = np.concatenate([np.ones((P, P), f), (token[:, None] <= token[None, :]).astype(f)], 1)
    triangle = np.where(token[None, :] > token[:, None], f(1e30), f(0))
    mask = np.concatenate([np.zeros((P, P), f), triangle, triangle], 1)
    half = ROPE // 2
    inv = (f(10000.0) ** (-np.arange(half, dtype=f) / f(half))).astype(f)
    angle = np.arange(SEQ, dtype=f)[:, None] * inv[None, :]
    dist = SEQ - 1 - np.arange(512)
    d = np.maximum(dist.astype(f), f(1.0))
    large = 16 + (np.log(d / f(16)) / f(math.log(128 / 16)) * f(16)).astype(np.int32)
    bucket = np.where(dist < 16, np.maximum(dist, 0), np.minimum(large, 31))
    onehot = -(np.arange(32)[:, None] == bucket[None, :]).astype(f)
    future = np.broadcast_to(np.where(dist < 0, f(1e30), f(0)), (A_HEADS, 512))
    return {"c_ident": np.eye(P, dtype=f), "c_upper": upper, "c_mask": mask.astype(f),
            "c_cos": np.cos(angle).astype(f), "c_sin": np.sin(angle).astype(f),
            "c_onehot": onehot, "c_future": np.ascontiguousarray(future, f)}


def kernel(**inputs):
    import numpy as np
    import concourse.bacc as bacc
    from concourse.bass_utils import run_bass_kernel_spmd

    nc = bacc.Bacc("TRN2", target_bir_lowering=False, num_devices=1)
    arrays, args = {}, []
    for name, a in [(n, np.ascontiguousarray(inputs[n])) for n in _INS] + list(constants().items()):
        arrays[f"in_{name}"] = a
        args.append(nc.dram_tensor(f"in_{name}", a.shape, mybir.dt.from_np(a.dtype), kind="ExternalInput").ap())
    out = nc.dram_tensor("out_x", (1, SEQ, D), mybir.dt.float32, kind="ExternalOutput").ap()
    program(nc, *args, out)
    r = run_bass_kernel_spmd(nc, [arrays], core_ids=[0])
    return r.results[0]["out_x"]
```

```python
import concourse.bass as bass
from concourse import mybir
from concourse.alu_op_type import AluOpType as ALU
from contextlib import ExitStack

P = 128
T = 2
SEQ = T * P
D = 1024
KD = D // P
FF = 2816
PAIRS = FF // 256
LAYERS = 2
RING = 3
UNIT = 2048
HALF = UNIT // 2
EPS = 1e-6
A_HEADS, A_DIM = 8, 64
B_HEADS, NOPE, ROPE, VDIM = 8, 64, 32, 64
Q_RANK, KV_RANK = 256, 128
QK_B = NOPE + ROPE
C_HEADS, C_DIM = 16, 64
AUG = 2
MLA_C = Q_RANK + KV_RANK + ROPE
HEADS = 16
BIG = 3.0e38

FFN_UNITS = 3 * PAIRS
AB1 = D
AB2 = 3 * A_HEADS * A_DIM + MLA_C - D
WIDTHS = []
START = {}


def _lay_out_units():
    def phase(name, widths):
        START[name] = len(WIDTHS)
        WIDTHS.extend(widths)
    for layer in range(LAYERS):
        phase(("ffn", 2 * layer), [UNIT] * FFN_UNITS)
        if layer == 0:
            phase("ab1", [2 * AB1] * 4)
            phase("ab2", [2 * AB2] * 4)
            phase("uq", [2 * B_HEADS * QK_B])
            phase("ukv", [B_HEADS * (NOPE + VDIM)])
        else:
            phase("fox_q", [UNIT] * 4)
            phase("fox_k", [UNIT] * 4)
            phase("fox_v", [UNIT] * 4)
            phase("fox_f", [KD * C_HEADS])
        phase(("out", layer), [UNIT] * 4)
        phase(("ffn", 2 * layer + 1), [UNIT] * FFN_UNITS)
        phase(("gate", layer), [UNIT] * 4)
        phase(("proj", layer), [UNIT])


_lay_out_units()
N_UNITS = len(WIDTHS)


def program(nc, x_in, p_in, t5_bias, ff1_norm, ff1_w_in, ff1_w_out, mix_norm, ff2_norm, ff2_w_in,
            ff2_w_out, ple_norm, ple_w_gate, ple_w_proj, ab_w_in, mla_q_norm, mla_w_uq,
            mla_kv_norm, mla_w_ukv, ab_w_out, fox_w_in, fox_b_f, fox_w_out, final_norm,
            c_ident, c_upper, c_mask, c_cos, c_sin, c_onehot, c_future, out):
    f32, f32r = mybir.dt.float32, mybir.dt.float32r
    ACT = mybir.ActivationFunctionType
    AX = mybir.AxisListType

    ctx = ExitStack()
    with ctx:
        def sb(name, shape, dt=f32):
            return ctx.enter_context(nc.sbuf_tensor(name, shape, dt))

        def sem(name):
            return ctx.enter_context(nc.semaphore(name))

        raw = sb("raw", [P, RING, UNIT])
        w_hi = sb("w_hi", [P, RING, UNIT], f32r)
        w_lo = sb("w_lo", [P, RING, UNIT], f32r)
        x = sb("x", [P, T, D])
        xg = sb("xg", [P, T, D])
        h_hi = sb("h_hi", [P, KD, SEQ], f32r)
        h_lo = sb("h_lo", [P, KD, SEQ], f32r)
        act_a = sb("act_a", [P, 512])
        hid = sb("hid", [P, 512])
        hid_hi = sb("hid_hi", [P, 2, SEQ], f32r)
        hid_lo = sb("hid_lo", [P, 2, SEQ], f32r)
        gain = sb("gain", [P, 2, D])
        meansq = sb("meansq", [P, T])
        minus_half = sb("minus_half", [P, 2 * T])
        rstd = sb("rstd", [P, T])
        half_rstd = sb("half_rstd", [P, T])
        q_rstd = sb("q_rstd", [P, T])
        junk = sb("junk", [P, D])
        diag = sb("diag", [P, T, P])
        rstd_row = sb("rstd_row", [P, SEQ])
        pT_hi = sb("pT_hi", [P, LAYERS, 2, SEQ], f32r)
        pT_lo = sb("pT_lo", [P, LAYERS, 2, SEQ], f32r)
        q_tok = sb("q_tok", [P, T, A_HEADS * A_DIM + B_HEADS * QK_B])
        k_tok = sb("k_tok", [P, T, D])
        v_tok = sb("v_tok", [P, T, D])
        comp = sb("comp", [P, T, MLA_C])
        comp_n = xg[:, :, 0:Q_RANK + KV_RANK]
        cT_hi = sb("cT_hi", [P, 3, SEQ], f32r)
        cT_lo = sb("cT_lo", [P, 3, SEQ], f32r)
        c_meansq = sb("c_meansq", [P, T, 2])
        c_rstd = sb("c_rstd", [P, T, 2])
        c_gain = sb("c_gain", [P, Q_RANK + KV_RANK])
        stage = sb("stage", [P, 2, 4, QK_B])
        qkT = sb("qkT", [P, 2, 512])
        neg_logits = sb("neg_logits", [P, 2, 384])
        neg_max = sb("neg_max", [P, 2, T])
        probs = sb("probs", [P, 2, 384])
        row_sum = sb("row_sum", [P, 2, T])
        row_inv = sb("row_inv", [P, 2, T])
        probsT = sb("probsT", [P, 2, 384])
        rope_t = sb("rope_t", [P, 4, B_HEADS, ROPE // 2])
        bias = sb("bias", [P, A_HEADS, 384])
        aug_q = sb("aug_q", [P, T, C_HEADS, AUG])
        aug_k = sb("aug_k", [P, T, C_HEADS, AUG])
        forget = sb("forget", [P, 5, T, C_HEADS])
        ident = sb("ident", [P, P])
        upper = sb("upper", [P, 2 * P])
        mask = sb("mask", [P, 384])
        cos = sb("cos", [P, T, ROPE // 2])
        sin = sb("sin", [P, T, ROPE // 2])
        t5_sb = sb("t5_sb", [32, A_HEADS])
        p_sb = k_tok[:, 1, :].rearrange("p (l t c) -> p l t c", l=LAYERS, t=T)
        t5_row, future, onehot = q_tok[0:A_HEADS, 0, 0:512], q_tok[0:A_HEADS, 0, 512:1024], k_tok[0:32, 0, 0:512]
        b_f = sb("b_f", [P, C_HEADS])
        t5_dram = nc.dram_tensor("t5_scratch", [A_HEADS, P, 512], f32, kind="Internal")

        bank = [ctx.enter_context(nc.psum_tensor(f"bank{i}", [P, 512], f32)) for i in range(8)]
        GATE, UP = bank[4], bank[5]

        raw_landed = [sem(f"raw_landed{s}") for s in range(RING)]
        hi_split = sem("hi_split")
        lo_split = sem("lo_split")
        unit_used = sem("unit_used")
        x_landed = sem("x_landed")
        ident_landed = sem("ident_landed")
        const_landed = sem("const_landed")
        t5_landed = sem("t5_landed")
        gain_landed = [sem("gain_landed0"), sem("gain_landed1")]
        x_ready = sem("x_ready")
        meansq_ready = sem("meansq_ready")
        rstd_ready = sem("rstd_ready")
        row_done = sem("row_done")
        row_copied = sem("row_copied")
        gate_scaled = sem("gate_scaled")
        root_step = sem("root_step")
        c_rstd_ready = sem("c_rstd_ready")
        xg_ready = sem("xg_ready")
        t_done = sem("t_done")
        h_hi_ready = sem("h_hi_ready")
        h_lo_ready = sem("h_lo_ready")
        y_part = sem("y_part")
        silu_done = sem("silu_done")
        hid_done = sem("hid_done")
        hid_hi_done = sem("hid_hi_done")
        hid_lo_done = sem("hid_lo_done")
        sig_done = sem("sig_done")
        gated = sem("gated")
        pT_done = sem("pT_done")
        pT_hi_done = sem("pT_hi_done")
        pT_lo_done = sem("pT_lo_done")
        t5_done = sem("t5_done")
        t5_row_done = sem("t5_row_done")
        t5_stored = sem("t5_stored")
        mix_act = sem("mix_act")
        mix_dve = sem("mix_dve")
        comp_sq = sem("comp_sq")
        comp_ready = sem("comp_ready")
        cT_done = sem("cT_done")
        cT_hi_done = sem("cT_hi_done")
        cT_lo_done = sem("cT_lo_done")
        rope_step = sem("rope_step")
        f_step = sem("f_step")
        f_act = sem("f_act")
        cum_done = sem("cum_done")
        aug_ready = sem("aug_ready")
        staged = sem("staged")
        qkT_done = sem("qkT_done")
        qkT_copied = sem("qkT_copied")
        logits_done = sem("logits_done")
        biased = sem("biased")
        max_done = sem("max_done")
        exp_done = sem("exp_done")
        probsT_done = sem("probsT_done")
        probsT_copied = sem("probsT_copied")
        inv_done = sem("inv_done")
        pv_done = sem("pv_done")
        head_done = sem("head_done")
        out_stored = sem("out_stored")

        def Y0(t):
            return [bank[2 * t][:, :], bank[2 * t + 1][:, :]]

        def Z0(t):
            return [bank[4 + 2 * t][:, :], bank[5 + 2 * t][:, :]]

        FINAL = 4 * LAYERS
        CONSTS = 11
        F_Z, F_ABS, F_EXP, F_LN, F_LOG = range(5)
        F_STEPS = 3
        PARTS = ((0, 0), (1, 0), (0, 1), (1, 1))
        norm_gain = []
        for layer in range(LAYERS):
            norm_gain += [ff1_norm[layer:layer + 1, :], mix_norm[layer:layer + 1, :],
                          ff2_norm[layer:layer + 1, :], ple_norm[layer:layer + 1, :]]
        norm_gain.append(final_norm.unsqueeze(0))

        def t_index(b):
            layer, k = divmod(b, 4)
            return 5 * layer + (k if k < 2 else k + 1)

        block = ctx.enter_context(nc.Block())

        @block.sync
        def _(sp):
            def load(n, source, i=0):
                if n >= RING:
                    sp.wait_ge(lo_split, 2 * (n - RING + 1) + 2 * RING * i)
                chunks = source.shape[1]
                sp.dma_start(raw[:, n % RING, 0:WIDTHS[n]].rearrange("p (k c) -> p k c", k=chunks),
                             source).then_inc(raw_landed[n % RING], 16)

            def rows(w, k0, nk, c0, width):
                return w[k0 * P:(k0 + nk) * P, c0:c0 + width].rearrange("(k p) c -> p k c", p=P)

            for b in range(T):
                sp.dma_start(x[:, b, :], x_in[0, b * P:(b + 1) * P, :]).then_inc(x_landed, 16)
            for layer in range(LAYERS):
                for half in range(2):
                    f = 2 * layer + half
                    w_in = (ff1_w_in, ff2_w_in)[half][layer, :, :].rearrange("(k p) c -> p k c", p=P)
                    w_out = (ff1_w_out, ff2_w_out)[half][layer, :, :].rearrange("(g p) c -> p g c", p=P)
                    n = START["ffn", f]

                    def gate_u(i):
                        return w_in[:, :, bass.ds(i * 256, 256)]

                    def up_u(i):
                        return w_in[:, :, bass.ds(i * 256 + FF, 256)]

                    def down_u(i):
                        return w_out[:, bass.ds(i * 2, 2), :]

                    load(n, gate_u(0))
                    load(n + 1, up_u(0))
                    load(n + 2, gate_u(1))
                    load(n + 3, down_u(0))
                    load(n + 4, up_u(1))
                    with sp.Fori(0, PAIRS - 3) as i:
                        load(n + 5, gate_u(i + 2), i)
                        load(n + 6, down_u(i + 1), i)
                        load(n + 7, up_u(i + 2), i)
                    load(n + 29, gate_u(PAIRS - 1))
                    load(n + 30, up_u(PAIRS - 1))
                    load(n + 31, down_u(PAIRS - 2))
                    load(n + 32, down_u(PAIRS - 1))
                    if half == 0 and layer == 0:
                        for j in range(4):
                            load(START["ab1"] + j, rows(ab_w_in[0], 2 * j, 2, 0, AB1))
                        for j in range(4):
                            load(START["ab2"] + j, rows(ab_w_in[0], 2 * j, 2, AB1, AB2))
                        load(START["uq"], rows(mla_w_uq[0], 0, 2, 0, B_HEADS * QK_B))
                        load(START["ukv"], rows(mla_w_ukv[0], 0, 1, 0, B_HEADS * (NOPE + VDIM)))
                    if half == 0 and layer == 1:
                        for c, name in enumerate(("fox_q", "fox_k", "fox_v")):
                            for j in range(4):
                                load(START[name] + j, rows(fox_w_in[0], 2 * j, 2, c * D, D))
                        with nc.allow_non_contiguous_dma(reason="sixteen columns of gates"):
                            load(START["fox_f"], rows(fox_w_in[0], 0, KD, 3 * D, C_HEADS))
                    if half == 0:
                        w = (ab_w_out, fox_w_out)[layer][0]
                        for j in range(4):
                            load(START["out", layer] + j, rows(w, 2 * j, 2, 0, D))
                for j in range(4):
                    load(START["gate", layer] + j, rows(ple_w_gate[layer], 2 * j, 2, 0, D))
                load(START["proj", layer], rows(ple_w_proj[layer], 0, 2, 0, D))
            for t in range(T):
                sp.wait_ge(xg_ready, 4 * FINAL + t + 1)
                sp.dma_start(out[0, t * P:(t + 1) * P, :], xg[:, t, :]).then_inc(out_stored, 16)
            sp.wait_ge(out_stored, 16 * T)

        @block.gpsimd
        def _(pool):
            pool.dma_start(gain[:, 0, :], norm_gain[0].partition_broadcast(P)).then_inc(gain_landed[0], 16)
            pool.dma_start(p_sb, p_in.rearrange("l b (t q) c -> q (l b) t c", q=P)).then_inc(const_landed, 16)
            pool.dma_start(upper[:, :], c_upper).then_inc(const_landed, 16)
            pool.dma_start(gain[:, 1, :], norm_gain[1].partition_broadcast(P)).then_inc(gain_landed[1], 16)
            pool.dma_start(t5_sb[:, :], t5_bias).then_inc(const_landed, 16)
            pool.dma_start(onehot, c_onehot).then_inc(const_landed, 16)
            pool.dma_start(future, c_future).then_inc(const_landed, 16)
            pool.dma_start(mask[:, :], c_mask).then_inc(const_landed, 16)
            pool.dma_start(cos[:, :, :], c_cos.rearrange("(t p) c -> p t c", p=P)).then_inc(const_landed, 16)
            pool.dma_start(sin[:, :, :], c_sin.rearrange("(t p) c -> p t c", p=P)).then_inc(const_landed, 16)
            pool.dma_start(c_gain[:, 0:Q_RANK], mla_q_norm.partition_broadcast(P)).then_inc(const_landed, 16)
            pool.dma_start(c_gain[:, Q_RANK:], mla_kv_norm.partition_broadcast(P)).then_inc(const_landed, 16)
            pool.dma_start(b_f[:, :], fox_b_f.partition_broadcast(P)).then_inc(const_landed, 16)
            def load_gain(b):
                pool.wait_ge(xg_ready, 4 * (b - 1))
                pool.dma_start(gain[:, b % 2, :], norm_gain[b].partition_broadcast(P)).then_inc(
                    gain_landed[b % 2], 16)

            roots = [0]

            def inverse_root(to, mean, exponent):
                nc.gpsimd.tensor_scalar(mean, mean, EPS, None, ALU.add).then_inc(root_step, 1)
                roots[0] += 1
                pool.wait_ge(root_step, roots[0])
                return nc.gpsimd.tensor_tensor(to, mean, exponent, ALU.pow)

            def rstds(b):
                for t in range(T):
                    pool.wait_ge(meansq_ready, T * b + t + 1)
                    last = inverse_root(rstd[:, t:t + 1], meansq[:, t:t + 1], minus_half[:, 0:1])
                if b % 4 in (1, 3) or b == FINAL:
                    if b % 4 == 1:
                        last.then_inc(root_step, 1)
                        roots[0] += 1
                        pool.wait_ge(root_step, roots[0])
                        last = nc.gpsimd.tensor_scalar(q_rstd[:, :], rstd[:, :], -A_DIM ** -0.5, None, ALU.mult)
                    last.then_inc(rstd_ready, 1)
                else:
                    last.then_inc(root_step, 1)
                    roots[0] += 1
                    pool.wait_ge(root_step, roots[0])
                    nc.gpsimd.tensor_scalar(half_rstd[:, :], rstd[:, :], 0.5, None, ALU.mult)
                    if b == 0:
                        pool.wait_ge(ident_landed, 16)
                    for t in range(T):
                        last = nc.gpsimd.tensor_scalar(diag[:, t, :], ident[:, :], rstd[:, t:t + 1], None, ALU.mult)
                    last.then_inc(rstd_ready, 1)

            def stage_head(h, count, kinds, d):
                s = count[0] % 2
                wait_h, hh = count[1], h
                if wait_h is not None:
                    pool.wait_ge(qkT_done, wait_h)
                last = len(kinds) - 1
                for j, (block0, width, at, source) in enumerate(kinds):
                    ins = nc.gpsimd.tensor_copy(stage[:, s, block0:block0 + T, at:at + width], source(hh))
                    if j == last:
                        ins.then_inc(staged, 1)

            def stage_heads(first, heads, kinds, d):
                for h in range(2):
                    stage_head(h, (first + h, first + h - 1 if first + h >= 2 else None), kinds, d)
                with pool.Fori(0, heads // 2 - 1) as i:
                    for s in range(2):
                        stage_head(i * 2 + (2 + s), (first + s, i * 2 + (first + s + 1)), kinds, d)

            nc.gpsimd.memset(stage[:, :, :, :], 0.0).then_inc(root_step, 1)
            roots[0] += 1
            nc.gpsimd.memset(minus_half[:, :], -0.5).then_inc(root_step, 1)
            roots[0] += 1
            rstds(0)
            load_gain(2)
            rstds(1)
            load_gain(3)
            pool.wait_ge(t5_row_done, 1)
            pool.dma_start(t5_dram.ap(), t5_row.unsqueeze(1).to_broadcast([A_HEADS, P, 512])).then_inc(t5_stored, 16)
            pool.wait_ge(t5_stored, 16)
            for c0, c1, ahead in ((0, SEQ, 0), (SEQ, 384, P)):
                toeplitz = bass.AP(tensor=t5_dram, offset=P - 1 + ahead,
                                   ap=[[511, P], [P * 512, A_HEADS], [1, c1 - c0]])
                pool.dma_start(bias[:, :, c0:c1], toeplitz).then_inc(t5_landed, 16)
            half = ROPE // 2
            steps = [0]

            def rope_op(out_, a, b, op):
                nc.gpsimd.tensor_tensor(out_, a, b, op).then_inc(rope_step, 1)
                steps[0] += 1

            def rotate(x1, x2, co, si, tmp):
                if steps[0]:
                    pool.wait_ge(rope_step, steps[0])
                rope_op(tmp[0], x1, co, ALU.mult)
                rope_op(tmp[1], x2, si, ALU.mult)
                rope_op(tmp[2], x1, si, ALU.mult)
                rope_op(tmp[3], x2, co, ALU.mult)
                pool.wait_ge(rope_step, steps[0])
                rope_op(x1, tmp[0], tmp[1], ALU.subtract)
                rope_op(x2, tmp[2], tmp[3], ALU.add)

            pool.wait_ge(comp_sq, 4)
            inverse_root(c_rstd[:, :, :].rearrange("p t c -> p (t c)"),
                         c_meansq[:, :, :].rearrange("p t c -> p (t c)"), minus_half[:, :]).then_inc(c_rstd_ready, 1)
            pool.wait_ge(mix_dve, 2)
            pool.wait_ge(const_landed, 16 * CONSTS)
            rotate(comp[:, :, Q_RANK + KV_RANK:Q_RANK + KV_RANK + half],
                   comp[:, :, Q_RANK + KV_RANK + half:MLA_C], cos[:, :, :], sin[:, :, :],
                   [rope_t[:, j, 0:T, :] for j in range(4)])
            pool.wait_ge(mix_act, 1)
            stage_heads(0, A_HEADS, [
                (0, A_DIM, 0, lambda h: q_tok[:, :, bass.ds(h * A_DIM, A_DIM)]),
                (2, A_DIM, 0, lambda h: k_tok[:, :, bass.ds(h * A_DIM, A_DIM)])], A_DIM)
            pool.wait_ge(mix_act, 4)
            pool.wait_ge(mix_dve, 4)
            q_b = q_tok[:, :, A_HEADS * A_DIM:].rearrange("p t (h c) -> p t h c", h=B_HEADS)
            for t in range(T):
                wide = [P, B_HEADS, half]
                rotate(q_b[:, t, :, NOPE:NOPE + half], q_b[:, t, :, NOPE + half:QK_B],
                       cos[:, t:t + 1, :].to_broadcast(wide), sin[:, t:t + 1, :].to_broadcast(wide),
                       [rope_t[:, j, :, :] for j in range(4)])
            pool.wait_ge(rope_step, steps[0])
            stage_heads(A_HEADS, B_HEADS, [
                (0, QK_B, 0, lambda h: q_tok[:, :, bass.ds(h * QK_B + A_HEADS * A_DIM, QK_B)]),
                (2, NOPE, 0, lambda h: k_tok[:, :, bass.ds(h * NOPE + A_HEADS * A_DIM, NOPE)]),
                (2, ROPE, NOPE, lambda h: comp[:, :, Q_RANK + KV_RANK:MLA_C])], QK_B)
            for b in range(2, 6):
                rstds(b)
                load_gain(b + 2)
            pool.wait_ge(aug_ready, 1)
            pool.wait_ge(mix_act, 6)
            stage_heads(HEADS, C_HEADS, [
                (0, C_DIM, 0, lambda h: q_tok[:, :, bass.ds(h * C_DIM, C_DIM)]),
                (2, C_DIM, 0, lambda h: k_tok[:, :, bass.ds(h * C_DIM, C_DIM)]),
                (0, AUG, C_DIM, lambda h: aug_q[:, :, bass.ds(h, 1), :].rearrange("p t h c -> p t (h c)")),
                (2, AUG, C_DIM, lambda h: aug_k[:, :, bass.ds(h, 1), :].rearrange("p t h c -> p t (h c)"))],
                C_DIM + AUG)
            for b in range(6, FINAL + 1):
                rstds(b)
                if b + 2 <= FINAL:
                    load_gain(b + 2)

        @block.tensor
        def _(pe):
            Y = [[bank[0], bank[1]], [bank[2], bank[3]]]
            Z = [[bank[4], bank[5]], [bank[6], bank[7]]]
            ROW = bank[7]

            def product(out_, a_hi, a_lo, b_hi, b_lo, start, stop):
                nc.tensor.matmul(out_, a_hi, b_hi, start=start, stop=False)
                nc.tensor.matmul(out_, a_hi, b_lo, start=False, stop=False)
                return nc.tensor.matmul(out_, a_lo, b_hi, start=False, stop=stop)

            def wide_unit(n, hi, lo, k0, banks, first, last, i=0):
                chunks = 1 if n == START["ukv"] else 2
                width = WIDTHS[n] // chunks
                s = n % RING
                pe.wait_ge(lo_split, i * (2 * RING) + 2 * (n + 1))
                for k in range(chunks):
                    for t in range(T):
                        for c in range((width + 511) // 512):
                            c0, c1 = k * width + 512 * c, k * width + min(512 * (c + 1), width)
                            ins = product(banks[t][c][:, 0:c1 - c0],
                                          hi[:, k0 + k, t * P:(t + 1) * P], lo[:, k0 + k, t * P:(t + 1) * P],
                                          w_hi[:, s, c0:c1], w_lo[:, s, c0:c1],
                                          start=first and k == 0, stop=last and k == chunks - 1)
                ins.then_inc(unit_used, 1)

            def transpose_part(source, part, banks):
                t, c = PARTS[part]
                for k in range(4):
                    ins = nc.tensor.transpose(banks[t][c][:, k * P:(k + 1) * P],
                                              source[:, t, c * 512 + k * P:c * 512 + (k + 1) * P], ident[:, :])
                ins.then_inc(t_done, 1)

            def closing_unit(n, hi, lo, k0, first, b):
                s, width = n % RING, WIDTHS[n] // 2
                pe.wait_ge(lo_split, 2 * (n + 1))
                for part, (t, c) in enumerate(PARTS):
                    for k in range(2):
                        c0 = k * width + 512 * c
                        ins = product(Y[t][c][:, :], hi[:, k0 + k, t * P:(t + 1) * P],
                                      lo[:, k0 + k, t * P:(t + 1) * P],
                                      w_hi[:, s, c0:c0 + 512], w_lo[:, s, c0:c0 + 512],
                                      start=first and k == 0, stop=k == 1)
                    ins.then_inc(y_part if part < 3 else unit_used, 1)
                    if part and b < FINAL:
                        pe.wait_ge(xg_ready, 4 * b + part)
                        transpose_part(xg, part - 1, Y)

            def last_part(b):
                pe.wait_ge(xg_ready, 4 * b + 4)
                transpose_part(xg, 3, Y)

            def narrow_unit(n, target, i=0, b=None):
                s = n % RING
                hi = w_hi[:, s, :].rearrange("p (k c) -> p k c", k=KD)
                lo = w_lo[:, s, :].rearrange("p (k c) -> p k c", k=KD)
                for k in range(KD):
                    if k == 0:
                        pe.wait_ge(lo_split, i * (2 * RING) + (2 * n + 1))
                    if k == KD // 2:
                        pe.wait_ge(lo_split, i * (2 * RING) + (2 * n + 2))
                    if b is not None and k == 0:
                        pe.wait_ge(h_lo_ready, 4 * t_index(b) + 2)
                    if b is not None and k == 2 and b > 0:
                        last_part(b)
                    if b is not None and k == KD // 2:
                        pe.wait_ge(h_lo_ready, 4 * t_index(b) + 4)
                    for g in range(2):
                        dst = target[:, g * SEQ:(g + 1) * SEQ]
                        w = slice(g * P, (g + 1) * P)
                        first, last = k == 0 and g == 0, k == KD - 1
                        nc.tensor.matmul(dst, hi[:, k, w], h_hi[:, k, :], start=first, stop=False,
                                         skip_group_check=True)
                        nc.tensor.matmul(dst, hi[:, k, w], h_lo[:, k, :], start=False, stop=False,
                                         skip_group_check=True)
                        ins = nc.tensor.matmul(dst, lo[:, k, w], h_hi[:, k, :], start=False, stop=last,
                                               skip_group_check=True)
                ins.then_inc(unit_used, 1)

            def ffn(f):
                n, p0 = START["ffn", f], PAIRS * f
                b = 4 * (f // 2) + 2 * (f % 2)

                def gate(n, pair, i=0, b=None):
                    if pair > 0:
                        pe.wait_ge(gate_scaled, i + pair)
                    narrow_unit(n, GATE, i, b)

                def up(n, pair, i=0):
                    if pair > 0:
                        pe.wait_ge(hid_done, i + pair)
                    narrow_unit(n, UP, i)

                def down(n, pair, i=0, first=False):
                    pe.wait_ge(hid_lo_done, i + (pair + 1))
                    wide_unit(n, hid_hi, hid_lo, 0, Y, first, False, i)

                gate(n, p0, 0, b)
                pe.wait_ge(rstd_ready, b + 1)
                if f == 0:
                    pe.wait_ge(const_landed, 16 * CONSTS)
                for t in range(T):
                    ins = nc.tensor.matmul(ROW[:, t * P:(t + 1) * P], upper[:, 0:P], diag[:, t, :], start=True,
                                           stop=True)
                ins.then_inc(row_done, 1)
                up(n + 1, p0)
                if f == 0:
                    transpose_embeddings(0, bank[6])
                gate(n + 2, p0 + 1)
                if f == 0:
                    pe.wait_ge(row_copied, 1)
                    transpose_embeddings(1, bank[7])
                down(n + 3, p0, first=True)
                if f == 0:
                    pe.wait_ge(pT_lo_done, 1)
                    nc.tensor.matmul(bank[6][0:A_HEADS, :], t5_sb[:, :], onehot, start=True,
                                     stop=True).then_inc(t5_done, 1)
                up(n + 4, p0 + 1)
                with pe.Fori(0, PAIRS - 3) as i:
                    gate(n + 5, p0 + 2, i)
                    down(n + 6, p0 + 1, i)
                    up(n + 7, p0 + 2, i)
                gate(n + 29, p0 + PAIRS - 1)
                up(n + 30, p0 + PAIRS - 1)
                down(n + 31, p0 + PAIRS - 2)
                pe.wait_ge(hid_lo_done, p0 + PAIRS)
                closing_unit(n + 32, cT_hi, cT_lo, 0, False, b + 1)

            def transpose_embeddings(layer, to):
                for k in range(2):
                    for t in range(T):
                        ins = nc.tensor.transpose(to[:, k * SEQ + t * P:k * SEQ + (t + 1) * P],
                                                  p_sb[:, layer, t, k * P:(k + 1) * P], ident[:, :])
                ins.then_inc(pT_done, 1)

            def project(name, banks, r=None, b=None, units=4):
                for j in range(units):
                    if r is not None and j in (0, 2):
                        pe.wait_ge(h_lo_ready, 4 * r + 2 + j)
                    wide_unit(START[name] + j, h_hi, h_lo, 2 * j, banks, j == 0, j == 3)
                    if b is not None and j == 0:
                        last_part(b)

            def attend(first, heads, d, dt):
                def transposes(h, s, i=None):
                    at = (lambda v: v) if i is None else (lambda v: i * 2 + v)
                    qk = bank[2 + s]
                    pe.wait_ge(staged, at(h + 1))
                    if h >= 2:
                        pe.wait_ge(qkT_copied, at(h - 1))
                    for j in range(4):
                        ins = nc.tensor.transpose(qk[0:dt, j * P:(j + 1) * P], stage[:, s, j, 0:dt], ident[:, :])
                    ins.then_inc(qkT_done, 1)

                def logits(h, s, i=None):
                    at = (lambda v: v) if i is None else (lambda v: i * 2 + v)
                    lg = bank[4 + s]
                    pe.wait_ge(qkT_copied, at(h + 1))
                    if h >= 2:
                        pe.wait_ge(biased, at(h - 1))
                    nc.tensor.matmul(lg[:, 0:SEQ], qkT[0:d, s, P:2 * P], qkT[0:d, s, 2 * P:4 * P],
                                     start=True, stop=True)
                    nc.tensor.matmul(lg[:, SEQ:SEQ + P], qkT[0:d, s, 0:P], qkT[0:d, s, 2 * P:3 * P],
                                     start=True, stop=True).then_inc(logits_done, 1)

                def probabilities(h, s, i=None):
                    at = (lambda v: v) if i is None else (lambda v: i * 2 + v)
                    pe.wait_ge(exp_done, at(h + 1))
                    if h >= 2:
                        pe.wait_ge(probsT_copied, at(h - 1))
                    for j in range(3):
                        ins = nc.tensor.transpose(bank[6 + s][:, j * P:(j + 1) * P],
                                                  probs[:, s, j * P:(j + 1) * P], ident[:, :])
                    ins.then_inc(probsT_done, 1)

                def values(h, s, i=None):
                    at = (lambda v: v) if i is None else (lambda v: i * 2 + v)
                    o = bank[s]
                    pe.wait_ge(probsT_copied, at(h + 1))
                    if h >= 2:
                        pe.wait_ge(head_done, at(h - 1))
                    col = h % HEADS * 64 if i is None else i * 128 + h % HEADS * 64
                    v = [v_tok[:, t, bass.ds(col, 64)] for t in range(T)]
                    nc.tensor.matmul(o[:, 0:64], probsT[:, s, 2 * P:3 * P], v[0], start=True, stop=True)
                    nc.tensor.matmul(o[:, 64:128], probsT[:, s, 0:P], v[0], start=True, stop=False)
                    nc.tensor.matmul(o[:, 64:128], probsT[:, s, P:2 * P], v[1], start=False,
                                     stop=True).then_inc(pv_done, 1)

                transposes(first, 0)
                transposes(first + 1, 1)
                logits(first, 0)
                transposes(first + 2, 0)
                logits(first + 1, 1)
                with pe.Fori(0, (heads - 4) // 2) as i:
                    for s in range(2):
                        transposes(first + 3 + s, 1 - s, i)
                        probabilities(first + s, s, i)
                        logits(first + 2 + s, s, i)
                        values(first + s, s, i)
                h = first + heads - 4
                for s in range(4):
                    if s == 0:
                        transposes(h + 3, 1)
                    probabilities(h + s, s % 2)
                    if s < 2:
                        logits(h + 2 + s, s)
                    values(h + s, s % 2)

            pe.wait_ge(ident_landed, 16)
            for part in range(4):
                pe.wait_ge(xg_ready, part + 1)
                transpose_part(xg, part, Y)
            for layer in range(LAYERS):
                b = 4 * layer
                ffn(2 * layer)
                if layer == 0:
                    pe.wait_ge(pT_lo_done, 2)
                    pe.wait_ge(t5_row_done, 1)
                    project("ab1", Z, t_index(b + 1), b + 1)
                    project("ab2", Y)
                    pe.wait_ge(mix_act, 1)
                    pe.wait_ge(mix_dve, 1)
                    for t in range(T):
                        pe.wait_ge(comp_ready, t + 1)
                        for k in range(3):
                            ins = nc.tensor.transpose(Z[t][0][:, k * P:(k + 1) * P],
                                                      comp_n[:, t, k * P:(k + 1) * P], ident[:, :])
                        ins.then_inc(cT_done, 1)
                    pe.wait_ge(cT_lo_done, 2)
                    wide_unit(START["uq"], cT_hi, cT_lo, 0, Z, True, True)
                    pe.wait_ge(mix_act, 2)
                    wide_unit(START["ukv"], cT_hi, cT_lo, 2, Y, True, True)
                    pe.wait_ge(mix_act, 4)
                    pe.wait_ge(mix_dve, 4)
                    attend(0, A_HEADS, A_DIM, QK_B)
                    attend(A_HEADS, B_HEADS, QK_B, QK_B)
                else:
                    project("fox_q", Z, t_index(b + 1), b + 1)
                    project("fox_k", Y)
                    pe.wait_ge(mix_act, 5)
                    pe.wait_ge(mix_dve, 5)
                    project("fox_v", Z)
                    pe.wait_ge(mix_dve, 6)
                    pe.wait_ge(mix_act, 6)
                    n = START["fox_f"]
                    pe.wait_ge(lo_split, 2 * (n + 1))
                    for t in range(T):
                        for k in range(KD):
                            cols = slice(k * C_HEADS, (k + 1) * C_HEADS)
                            ins = product(bank[0][:, t * C_HEADS:(t + 1) * C_HEADS],
                                          h_hi[:, k, t * P:(t + 1) * P], h_lo[:, k, t * P:(t + 1) * P],
                                          w_hi[:, n % RING, cols], w_lo[:, n % RING, cols],
                                          start=k == 0, stop=k == KD - 1)
                    ins.then_inc(unit_used, 1)
                    pe.wait_ge(f_step, F_STEPS)
                    lf = forget[:, F_LOG, :, :]
                    nc.tensor.matmul(bank[1][:, 0:C_HEADS], upper[:, P:2 * P], lf[:, 0, :], start=True, stop=True)
                    nc.tensor.matmul(bank[1][:, C_HEADS:2 * C_HEADS], upper[:, 0:P], lf[:, 0, :], start=True,
                                     stop=False)
                    nc.tensor.matmul(bank[1][:, C_HEADS:2 * C_HEADS], upper[:, P:2 * P], lf[:, 1, :],
                                     start=False, stop=True).then_inc(cum_done, 1)
                    pe.wait_ge(mix_act, 7)
                    pe.wait_ge(mix_dve, 7)
                    pe.wait_ge(aug_ready, 1)
                    attend(HEADS, C_HEADS, C_DIM + AUG, C_DIM + AUG)
                pe.wait_ge(head_done, HEADS * (layer + 1))
                for part in range(4):
                    transpose_part(xg, part, Z)
                r = 5 * layer + 2
                project(("out", layer), Y, r, units=3)
                closing_unit(START["out", layer] + 3, h_hi, h_lo, 6, False, b + 2)
                ffn(2 * layer + 1)
                project(("gate", layer), Z, t_index(b + 3), b + 3)
                closing_unit(START["proj", layer], pT_hi[:, layer, :, :], pT_lo[:, layer, :, :], 0, True, b + 4)

        @block.scalar
        def _(act):
            def split(n, i=0):
                if n >= N_UNITS:
                    return
                s, half = n % RING, WIDTHS[n] // 2
                act.wait_ge(raw_landed[s], 16 * (n // RING + 1) + i * 16)
                if n >= RING:
                    act.wait_ge(unit_used, i * RING + (n - RING + 1))
                for j in range(2):
                    cols = slice(j * half, (j + 1) * half)
                    nc.scalar.copy(w_hi[:, s, cols], raw[:, s, cols]).then_inc(hi_split, 1)

            def splits_behind(name, count):
                for j in range(count):
                    split(START[name] + j + RING - 1)

            def mean_square(b, t):
                if b == 0:
                    act.wait_ge(x_landed, 16 * T)
                else:
                    act.wait_ge(x_ready, 4 * (b - 1) + 3 + t)
                if b or t:
                    act.wait_ge(meansq_ready, T * b + t)
                nc.scalar.activation(junk[:, :], x[:, t, :], ACT.Square, scale=D ** -0.5,
                                     accum_out=meansq[:, t:t + 1]).then_inc(meansq_ready, 1)

            def input_hi(r, part, first_bank=0):
                act.wait_ge(t_done, 4 * r + part + 1)
                t, c = PARTS[part]
                nc.scalar.copy(h_hi[:, 4 * c:4 * c + 4, t * P:(t + 1) * P],
                               bank[first_bank + 2 * t + c][:, :].rearrange("p (k c) -> p k c", k=4)).then_inc(
                                   h_hi_ready, 1)

            def next_input(b):
                r = t_index(b)
                input_hi(r, 0)
                input_hi(r, 1)
                mean_square(b, 0)
                input_hi(r, 2)
                mean_square(b, 1)
                input_hi(r, 3)

            def ffn(f):
                n, p0 = START["ffn", f], PAIRS * f

                def silu(pair, i=0):
                    act.wait_ge(gate_scaled, i + (pair + 1))
                    nc.scalar.activation(act_a[:, :], act_a[:, :], ACT.Silu).then_inc(silu_done, 1)

                def hidden_hi(pair, i=0, to=hid_hi):
                    act.wait_ge(hid_done, i + (pair + 1))
                    nc.scalar.copy(to[:, 0:2, :], hid[:, :].rearrange("p (g c) -> p g c", g=2)).then_inc(
                        hid_hi_done, 1)

                def embedding_hi(layer):
                    act.wait_ge(pT_done, layer + 1)
                    nc.scalar.copy(pT_hi[:, layer, :, :], bank[6 + layer][:, :].rearrange(
                        "p (k c) -> p k c", k=2)).then_inc(pT_hi_done, 1)

                split(n + 2)
                act.wait_ge(row_done, f + 1)
                nc.scalar.copy(rstd_row[:, :], bank[7][:, 0:SEQ]).then_inc(row_copied, 1)
                silu(p0)
                split(n + 3)
                hidden_hi(p0)
                if f == 0:
                    embedding_hi(0)
                split(n + 4)
                silu(p0 + 1)
                if f == 0:
                    embedding_hi(1)
                split(n + 5)
                split(n + 6)
                hidden_hi(p0 + 1)
                with act.Fori(0, PAIRS - 3) as i:
                    split(n + 7, i)
                    silu(p0 + 2, i)
                    split(n + 8, i)
                    split(n + 9, i)
                    hidden_hi(p0 + 2, i)
                split(n + 31)
                silu(p0 + PAIRS - 1)
                split(n + 32)
                hidden_hi(p0 + PAIRS - 1, 0, cT_hi)
                split(n + 33)
                split(n + 34)

            def attend(first, heads, d):
                def copy_qkT(h, s, at):
                    act.wait_ge(qkT_done, at(h + 1))
                    if h >= 2:
                        act.wait_ge(logits_done, at(h - 1))
                    nc.scalar.copy(qkT[0:d, s, :], bank[2 + s][0:d, :]).then_inc(qkT_copied, 1)

                def exps(h, s, at):
                    act.wait_ge(max_done, at(h + 1))
                    if h >= 2:
                        act.wait_ge(probsT_done, at(h - 1))
                        act.wait_ge(inv_done, at(h - 1))
                    nc.scalar.activation(probs[:, s, 0:SEQ], neg_logits[:, s, 0:SEQ], ACT.Exp, scale=-1.0,
                                         bias=neg_max[:, s, 1:2], accum_out=row_sum[:, s, 1:2])
                    nc.scalar.activation(probs[:, s, SEQ:], neg_logits[:, s, SEQ:], ACT.Exp, scale=-1.0,
                                         bias=neg_max[:, s, 0:1], accum_out=row_sum[:, s, 0:1]).then_inc(exp_done, 1)

                for s in range(3):
                    copy_qkT(first + s, s % 2, lambda v: v)
                with act.Fori(0, (heads - 4) // 2) as i:
                    for s in range(2):
                        exps(first + s, s, lambda v: i * 2 + v)
                        copy_qkT(first + 3 + s, 1 - s, lambda v: i * 2 + v)
                h = first + heads - 4
                exps(h, 0, lambda v: v)
                copy_qkT(h + 3, 1, lambda v: v)
                for s in range(1, 4):
                    exps(h + s, s % 2, lambda v: v)

            act.dma_start(ident[:, :], c_ident).then_inc(ident_landed, 16)
            mean_square(0, 0)
            mean_square(0, 1)
            for part in range(4):
                input_hi(0, part)
            for n in range(RING - 1):
                split(n)
            for layer in range(LAYERS):
                b = 4 * layer
                ffn(2 * layer)
                next_input(b + 1)
                if layer == 0:
                    splits_behind("ab1", 4)
                    act.wait_ge(rstd_ready, b + 2)
                    act.wait_ge(unit_used, START["ab1"] + 4)
                    act.wait_ge(t5_stored, 16)
                    for t in range(T):
                        ins = nc.scalar.mul(q_tok[:, t, 0:512], Z0(t)[0], q_rstd[:, t:t + 1])
                    ins.then_inc(mix_act, 1)
                    splits_behind("ab2", 3)
                    act.wait_ge(unit_used, START["ab2"] + 4)
                    for t in range(T):
                        ins = nc.scalar.mul(v_tok[:, t, 0:512], Y0(t)[0], rstd[:, t:t + 1])
                    ins.then_inc(mix_act, 1)
                    act.wait_ge(mix_dve, 2)
                    for t in range(T):
                        for j, (c0, c1) in enumerate(((0, Q_RANK), (Q_RANK, Q_RANK + KV_RANK))):
                            ins = nc.scalar.activation(comp_n[:, t, c0:c1], comp[:, t, c0:c1], ACT.Square,
                                                       scale=(c1 - c0) ** -0.5,
                                                       accum_out=c_meansq[:, t, j:j + 1])
                            ins.then_inc(comp_sq, 1)
                    split(START["ab2"] + 3 + RING - 1)
                    for t in range(T):
                        act.wait_ge(cT_done, t + 1)
                        nc.scalar.copy(cT_hi[:, :, t * P:(t + 1) * P],
                                       Z0(t)[0][:, 0:3 * P].rearrange("p (k c) -> p k c", k=3)).then_inc(
                                           cT_hi_done, 1)
                    splits_behind("uq", 1)
                    act.wait_ge(unit_used, START["uq"] + 1)
                    for t in range(T):
                        ins = nc.scalar.mul(q_tok[:, t, 512:1024], Z0(t)[0], -QK_B ** -0.5)
                    ins.then_inc(mix_act, 1)
                    act.wait_ge(unit_used, START["ukv"] + 1)
                    for t in range(T):
                        kv = Y0(t)[0].rearrange("p (h c) -> p h c", h=4)
                        nc.scalar.copy(k_tok[:, t, 512:768].rearrange("p (h c) -> p h c", h=4), kv[:, :, 0:NOPE])
                        ins = nc.scalar.copy(v_tok[:, t, 512:768].rearrange("p (h c) -> p h c", h=4),
                                             kv[:, :, NOPE:])
                    ins.then_inc(mix_act, 1)
                    splits_behind("ukv", 1)
                    attend(0, A_HEADS, QK_B)
                    attend(A_HEADS, B_HEADS, QK_B)
                else:
                    splits_behind("fox_q", 4)
                    act.wait_ge(rstd_ready, b + 2)
                    act.wait_ge(unit_used, START["fox_q"] + 4)
                    for t in range(T):
                        ins = nc.scalar.mul(q_tok[:, t, 0:512], Z0(t)[0], q_rstd[:, t:t + 1])
                    ins.then_inc(mix_act, 1)
                    splits_behind("fox_k", 4)
                    act.wait_ge(unit_used, START["fox_k"] + 4)
                    for t in range(T):
                        ins = nc.scalar.mul(k_tok[:, t, 0:512], Y0(t)[0], rstd[:, t:t + 1])
                    ins.then_inc(mix_act, 1)
                    splits_behind("fox_v", 4)
                    act.wait_ge(unit_used, START["fox_v"] + 4)
                    for t in range(T):
                        ins = nc.scalar.mul(v_tok[:, t, 0:512], Z0(t)[0], rstd[:, t:t + 1])
                    ins.then_inc(mix_act, 1)
                    splits_behind("fox_f", 1)
                    act.wait_ge(f_step, 2)
                    nc.scalar.activation(forget[:, F_EXP, :, :], forget[:, F_ABS, :, :], ACT.Exp,
                                         scale=-1.0).then_inc(f_act, 1)
                    act.wait_ge(f_act, 1)
                    nc.scalar.activation(forget[:, F_LN, :, :], forget[:, F_EXP, :, :], ACT.Ln,
                                         bias=1.0).then_inc(f_act, 1)
                    attend(HEADS, C_HEADS, C_DIM + AUG)
                for part in range(4):
                    input_hi(5 * layer + 2, part, 4)
                splits_behind(("out", layer), 4)
                next_input(b + 2)
                ffn(2 * layer + 1)
                next_input(b + 3)
                splits_behind(("gate", layer), 4)
                act.wait_ge(rstd_ready, b + 4)
                act.wait_ge(unit_used, START["gate", layer] + 4)
                for t, c in PARTS:
                    nc.scalar.activation(xg[:, t, 512 * c:512 * (c + 1)], Z0(t)[c],
                                         ACT.Sigmoid, scale=rstd[:, t:t + 1]).then_inc(sig_done, 1)
                splits_behind(("proj", layer), 1)
                if layer + 1 < LAYERS:
                    next_input(b + 4)
            mean_square(FINAL, 0)
            mean_square(FINAL, 1)

        @block.vector
        def _(dve):
            def split(n, i=0):
                if n >= N_UNITS:
                    return
                s, half = n % RING, WIDTHS[n] // 2
                for j in range(2):
                    dve.wait_ge(hi_split, i * (2 * RING) + (2 * n + j + 1))
                    cols = slice(j * half, (j + 1) * half)
                    nc.vector.tensor_tensor(w_lo[:, s, cols], raw[:, s, cols], w_hi[:, s, cols].bitcast(f32),
                                            ALU.subtract).then_inc(lo_split, 1)

            def splits_behind(name, count):
                for j in range(count):
                    split(START[name] + j + RING - 1)

            def times_gain(b, part):
                t, c = PARTS[part]
                cols = slice(512 * c, 512 * (c + 1))
                nc.vector.tensor_tensor(xg[:, t, cols], x[:, t, cols], gain[:, b % 2, cols],
                                        ALU.mult).then_inc(xg_ready, 1)

            def input_lo(r, part, first_bank=0):
                dve.wait_ge(h_hi_ready, 4 * r + part + 1)
                t, c = PARTS[part]
                to = slice(4 * c, 4 * c + 4), slice(t * P, (t + 1) * P)
                nc.vector.tensor_tensor(h_lo[:, to[0], to[1]],
                                        bank[first_bank + 2 * t + c][:, :].rearrange("p (k c) -> p k c", k=4),
                                        h_hi[:, to[0], to[1]].bitcast(f32), ALU.subtract).then_inc(h_lo_ready, 1)

            sums = [0]

            def next_input(b, closing, factor):
                for part, (t, c) in enumerate(PARTS):
                    cols = slice(512 * c, 512 * (c + 1))
                    if factor is None:
                        dve.wait_ge(sig_done, 4 * (b // 4 - 1) + part + 1)
                    if part < 3:
                        sums[0] += 1
                        dve.wait_ge(y_part, sums[0])
                    else:
                        dve.wait_ge(unit_used, closing + 1)
                    if factor is None:
                        nc.vector.tensor_tensor(xg[:, t, cols], xg[:, t, cols], bank[2 * t + c][:, :],
                                                ALU.mult).then_inc(gated, 1)
                        dve.wait_ge(gated, 4 * (b // 4 - 1) + part + 1)
                        nc.vector.tensor_tensor(x[:, t, cols], x[:, t, cols], xg[:, t, cols],
                                                ALU.add).then_inc(x_ready, 1)
                    else:
                        nc.vector.scalar_tensor_tensor(x[:, t, cols], bank[2 * t + c][:, :], factor(t),
                                                       x[:, t, cols], ALU.mult, ALU.add).then_inc(x_ready, 1)
                    if b < FINAL:
                        dve.wait_ge(x_ready, 4 * (b - 1) + part + 1)
                        if part == 0:
                            dve.wait_ge(gain_landed[b % 2], 16 * (b // 2 + 1))
                        times_gain(b, part)
                        if part:
                            input_lo(t_index(b), part - 1)
                if b < FINAL:
                    input_lo(t_index(b), 3)

            def ffn(f):
                n, p0 = START["ffn", f], PAIRS * f
                b = 4 * (f // 2) + 2 * (f % 2)

                def scale_gate(n, pair, i=0):
                    dve.wait_ge(unit_used, i * RING + (n + 1))
                    nc.vector.tensor_tensor(act_a[:, :].rearrange("p (g c) -> p g c", g=2),
                                            GATE[:, :].rearrange("p (g c) -> p g c", g=2),
                                            rstd_row[:, :].unsqueeze(1).to_broadcast([P, 2, SEQ]),
                                            ALU.mult).then_inc(gate_scaled, 1)

                def hidden(n, pair, i=0, hi=hid_hi, lo=hid_lo):
                    dve.wait_ge(silu_done, i + (pair + 1))
                    dve.wait_ge(unit_used, i * RING + (n + 1))
                    nc.vector.tensor_tensor(hid[:, :], act_a[:, :], UP[:, :], ALU.mult).then_inc(hid_done, 1)
                    dve.wait_ge(hid_hi_done, i + (pair + 1))
                    nc.vector.tensor_tensor(lo[:, 0:2, :], hid[:, :].rearrange("p (g c) -> p g c", g=2),
                                            hi[:, 0:2, :].bitcast(f32), ALU.subtract).then_inc(hid_lo_done, 1)

                def embedding_lo(layer):
                    dve.wait_ge(pT_hi_done, layer + 1)
                    nc.vector.tensor_tensor(pT_lo[:, layer, :, :],
                                            bank[6 + layer][:, :].rearrange("p (k c) -> p k c", k=2),
                                            pT_hi[:, layer, :, :].bitcast(f32), ALU.subtract).then_inc(pT_lo_done, 1)

                split(n + 2)
                dve.wait_ge(row_copied, f + 1)
                scale_gate(n, p0)
                split(n + 3)
                hidden(n + 1, p0)
                if f == 0:
                    embedding_lo(0)
                split(n + 4)
                scale_gate(n + 2, p0 + 1)
                if f == 0:
                    embedding_lo(1)
                split(n + 5)
                if f == 0:
                    dve.wait_ge(const_landed, 16 * CONSTS)
                    dve.wait_ge(t5_done, 1)
                    nc.vector.tensor_tensor(t5_row, future, bank[6][0:A_HEADS, :], ALU.add).then_inc(t5_row_done, 1)
                split(n + 6)
                hidden(n + 4, p0 + 1)
                with dve.Fori(0, PAIRS - 3) as i:
                    split(n + 7, i)
                    scale_gate(n + 5, p0 + 2, i)
                    split(n + 8, i)
                    split(n + 9, i)
                    hidden(n + 7, p0 + 2, i)
                split(n + 31)
                scale_gate(n + 29, p0 + PAIRS - 1)
                split(n + 32)
                hidden(n + 30, p0 + PAIRS - 1, 0, cT_hi, cT_lo)
                split(n + 33)
                next_input(b + 1, n + 32, lambda t: half_rstd[:, t:t + 1])
                split(n + 34)

            def attend(first, heads, negated_bias):
                def maxima(h, s, at, head):
                    dve.wait_ge(logits_done, at(h + 1))
                    if h >= 2:
                        dve.wait_ge(exp_done, at(h - 1))
                    nc.vector.tensor_tensor(neg_logits[:, s, :], negated_bias(head), bank[4 + s][:, 0:384],
                                            ALU.add).then_inc(biased, 1)
                    dve.wait_ge(biased, at(h + 1))
                    nc.vector.tensor_reduce(neg_max[:, s, 1:2], neg_logits[:, s, 0:SEQ], AX.X, ALU.min)
                    nc.vector.tensor_reduce(neg_max[:, s, 0:1], neg_logits[:, s, SEQ:], AX.X,
                                            ALU.min).then_inc(max_done, 1)

                def copy_probsT(h, s, at):
                    dve.wait_ge(exp_done, at(h + 1))
                    nc.vector.reciprocal(row_inv[:, s, :], row_sum[:, s, :]).then_inc(inv_done, 1)
                    dve.wait_ge(probsT_done, at(h + 1))
                    if h >= 2:
                        dve.wait_ge(pv_done, at(h - 1))
                    nc.vector.tensor_copy(probsT[:, s, :], bank[6 + s][:, 0:384]).then_inc(probsT_copied, 1)

                def output(h, s, at, column):
                    dve.wait_ge(pv_done, at(h + 1))
                    dve.wait_ge(inv_done, at(h + 1))
                    nc.vector.tensor_tensor(xg[:, :, bass.ds(column, 64)],
                                            bank[s][:, 0:P].rearrange("p (t c) -> p t c", t=T),
                                            row_inv[:, s, :].unsqueeze(2).to_broadcast([P, T, 64]),
                                            ALU.mult).then_inc(head_done, 1)

                f0 = first % HEADS
                for s in range(2):
                    maxima(first + s, s, lambda v: v, s)
                with dve.Fori(0, (heads - 4) // 2) as i:
                    for s in range(2):
                        at = lambda v: i * 2 + v
                        copy_probsT(first + s, s, at)
                        maxima(first + 2 + s, s, at, i * 2 + (2 + s))
                        output(first + s, s, at, i * 128 + (f0 + s) * 64)
                for s in range(heads - 4, heads):
                    copy_probsT(first + s, s % 2, lambda v: v)
                    if s < heads - 2:
                        maxima(first + 2 + s, s % 2, lambda v: v, s + 2)
                    output(first + s, s % 2, lambda v: v, (f0 + s) * 64)

            dve.wait_ge(x_landed, 16 * T)
            dve.wait_ge(gain_landed[0], 16)
            for part in range(4):
                times_gain(0, part)
            for part in range(4):
                input_lo(0, part)
            for n in range(RING - 1):
                split(n)
            for layer in range(LAYERS):
                b = 4 * layer
                ffn(2 * layer)
                if layer == 0:
                    splits_behind("ab1", 4)
                    dve.wait_ge(rstd_ready, b + 2)
                    dve.wait_ge(unit_used, START["ab1"] + 4)
                    for t in range(T):
                        ins = nc.vector.tensor_scalar(k_tok[:, t, 0:512], Z0(t)[1], rstd[:, t:t + 1], None, ALU.mult)
                    ins.then_inc(mix_dve, 1)
                    splits_behind("ab2", 3)
                    dve.wait_ge(unit_used, START["ab2"] + 4)
                    for t in range(T):
                        ins = nc.vector.tensor_scalar(comp[:, t, :], Y0(t)[1][:, 0:MLA_C], rstd[:, t:t + 1], None,
                                                      ALU.mult)
                    ins.then_inc(mix_dve, 1)
                    dve.wait_ge(c_rstd_ready, 1)
                    for t in range(T):
                        for j, (c0, c1) in enumerate(((0, Q_RANK), (Q_RANK, Q_RANK + KV_RANK))):
                            ins = nc.vector.scalar_tensor_tensor(comp_n[:, t, c0:c1], comp[:, t, c0:c1],
                                                                 c_rstd[:, t, j:j + 1], c_gain[:, c0:c1],
                                                                 ALU.mult, ALU.mult)
                        ins.then_inc(comp_ready, 1)
                    split(START["ab2"] + 3 + RING - 1)
                    for t in range(T):
                        dve.wait_ge(cT_hi_done, t + 1)
                        nc.vector.tensor_tensor(cT_lo[:, :, t * P:(t + 1) * P],
                                                Z0(t)[0][:, 0:3 * P].rearrange("p (k c) -> p k c", k=3),
                                                cT_hi[:, :, t * P:(t + 1) * P].bitcast(f32),
                                                ALU.subtract).then_inc(cT_lo_done, 1)
                    splits_behind("uq", 1)
                    dve.wait_ge(unit_used, START["uq"] + 1)
                    for t in range(T):
                        ins = nc.vector.tensor_scalar(q_tok[:, t, 1024:1280], Z0(t)[1][:, 0:256],
                                                      -QK_B ** -0.5, None, ALU.mult)
                    ins.then_inc(mix_dve, 1)
                    dve.wait_ge(unit_used, START["ukv"] + 1)
                    for t in range(T):
                        kv = Y0(t)[1].rearrange("p (h c) -> p h c", h=4)
                        nc.vector.tensor_copy(k_tok[:, t, 768:1024].rearrange("p (h c) -> p h c", h=4),
                                              kv[:, :, 0:NOPE])
                        ins = nc.vector.tensor_copy(v_tok[:, t, 768:1024].rearrange("p (h c) -> p h c", h=4),
                                                    kv[:, :, NOPE:])
                    ins.then_inc(mix_dve, 1)
                    splits_behind("ukv", 1)
                    dve.wait_ge(t5_landed, 32)
                    attend(0, A_HEADS, lambda h: bias[:, bass.ds(h, 1), :].rearrange("p h c -> p (h c)"))
                    attend(A_HEADS, B_HEADS, lambda h: mask[:, :])
                else:
                    splits_behind("fox_q", 4)
                    dve.wait_ge(rstd_ready, b + 2)
                    dve.wait_ge(unit_used, START["fox_q"] + 4)
                    for t in range(T):
                        ins = nc.vector.tensor_scalar(q_tok[:, t, 512:1024], Z0(t)[1], q_rstd[:, t:t + 1], None,
                                                      ALU.mult)
                    ins.then_inc(mix_dve, 1)
                    splits_behind("fox_k", 4)
                    dve.wait_ge(unit_used, START["fox_k"] + 4)
                    for t in range(T):
                        ins = nc.vector.tensor_scalar(k_tok[:, t, 512:1024], Y0(t)[1], rstd[:, t:t + 1], None,
                                                      ALU.mult)
                    ins.then_inc(mix_dve, 1)
                    splits_behind("fox_v", 4)
                    dve.wait_ge(unit_used, START["fox_v"] + 4)
                    for t in range(T):
                        ins = nc.vector.tensor_scalar(v_tok[:, t, 512:1024], Z0(t)[1], rstd[:, t:t + 1], None,
                                                      ALU.mult)
                    ins.then_inc(mix_dve, 1)
                    fsteps = [0]

                    def f_next(ins):
                        ins.then_inc(f_step, 1)
                        fsteps[0] += 1
                        dve.wait_ge(f_step, fsteps[0])

                    dve.wait_ge(unit_used, START["fox_f"] + 1)
                    z = forget[:, F_Z, :, :]
                    for t in range(T):
                        last = nc.vector.scalar_tensor_tensor(z[:, t, :], bank[0][:, t * C_HEADS:(t + 1) * C_HEADS],
                                                              rstd[:, t:t + 1], b_f[:, :], ALU.mult, ALU.add)
                    f_next(last)
                    f_next(nc.vector.scalar_tensor_tensor(forget[:, F_ABS, :, :], z, -1.0, z, ALU.mult, ALU.max))
                    splits_behind("fox_f", 1)
                    dve.wait_ge(f_act, 2)
                    f_next(nc.vector.scalar_tensor_tensor(forget[:, F_LOG, :, :], z, 0.0, forget[:, F_LN, :, :],
                                                          ALU.min, ALU.subtract))
                    dve.wait_ge(cum_done, 1)
                    cum = bank[1][:, 0:T * C_HEADS].rearrange("p (t h) -> p t h", t=T)
                    nc.vector.memset(aug_q[:, :, :, 0], -1.0)
                    nc.vector.memset(aug_k[:, :, :, 1], 1.0)
                    nc.vector.tensor_scalar(aug_q[:, :, :, 1], cum, -1.0, None, ALU.mult)
                    nc.vector.tensor_scalar(aug_k[:, :, :, 0], cum, -1.0, None, ALU.mult).then_inc(aug_ready, 1)
                    attend(HEADS, C_HEADS, lambda h: mask[:, :])
                for part in range(4):
                    input_lo(5 * layer + 2, part, 4)
                splits_behind(("out", layer), 3)
                next_input(b + 2, START["out", layer] + 3, lambda t: 1.0)
                split(START["out", layer] + 3 + RING - 1)
                ffn(2 * layer + 1)
                splits_behind(("gate", layer), 4)
                next_input(b + 4, START["proj", layer], None)
                splits_behind(("proj", layer), 1)
            dve.wait_ge(gain_landed[FINAL % 2], 16 * (FINAL // 2 + 1))
            dve.wait_ge(rstd_ready, FINAL + 1)
            for t in range(T):
                nc.vector.scalar_tensor_tensor(xg[:, t, :], x[:, t, :], rstd[:, t:t + 1], gain[:, FINAL % 2, :],
                                               ALU.mult, ALU.mult).then_inc(xg_ready, 1)


_INS = ["x", "p", "t5_bias", "ff1_norm", "ff1_w_in", "ff1_w_out", "mix_norm", "ff2_norm", "ff2_w_in",
        "ff2_w_out", "ple_norm", "ple_w_gate", "ple_w_proj", "ab_w_in", "mla_q_norm", "mla_w_uq",
        "mla_kv_norm", "mla_w_ukv", "ab_w_out", "fox_w_in", "fox_b_f", "fox_w_out", "final_norm"]


def constants():
    import math
    import numpy as np
    f = np.float32
    token = np.arange(P)
    upper = np.concatenate([np.ones((P, P), f), (token[:, None] <= token[None, :]).astype(f)], 1)
    triangle = np.where(token[None, :] > token[:, None], f(1e30), f(0))
    mask = np.concatenate([np.zeros((P, P), f), triangle, triangle], 1)
    half = ROPE // 2
    inv = (f(10000.0) ** (-np.arange(half, dtype=f) / f(half))).astype(f)
    angle = np.arange(SEQ, dtype=f)[:, None] * inv[None, :]
    dist = SEQ - 1 - np.arange(512)
    d = np.maximum(dist.astype(f), f(1.0))
    large = 16 + (np.log(d / f(16)) / f(math.log(128 / 16)) * f(16)).astype(np.int32)
    bucket = np.where(dist < 16, np.maximum(dist, 0), np.minimum(large, 31))
    onehot = -(np.arange(32)[:, None] == bucket[None, :]).astype(f)
    future = np.broadcast_to(np.where(dist < 0, f(1e30), f(0)), (A_HEADS, 512))
    return {"c_ident": np.eye(P, dtype=f), "c_upper": upper, "c_mask": mask.astype(f),
            "c_cos": np.cos(angle).astype(f), "c_sin": np.sin(angle).astype(f),
            "c_onehot": onehot, "c_future": np.ascontiguousarray(future, f)}


def kernel(**inputs):
    import numpy as np
    import concourse.bacc as bacc
    from concourse.bass_utils import run_bass_kernel_spmd

    nc = bacc.Bacc("TRN2", target_bir_lowering=False, num_devices=1)
    arrays, args = {}, []
    for name, a in [(n, np.ascontiguousarray(inputs[n])) for n in _INS] + list(constants().items()):
        arrays[f"in_{name}"] = a
        args.append(nc.dram_tensor(f"in_{name}", a.shape, mybir.dt.from_np(a.dtype), kind="ExternalInput").ap())
    out = nc.dram_tensor("out_x", (1, SEQ, D), mybir.dt.float32, kind="ExternalOutput").ap()
    program(nc, *args, out)
    r = run_bass_kernel_spmd(nc, [arrays], core_ids=[0])
    return r.results[0]["out_x"]
```

```python
import concourse.bass as bass
from concourse import mybir
from concourse.alu_op_type import AluOpType as ALU
from contextlib import ExitStack

P = 128
T = 2
SEQ = T * P
D = 1024
KD = D // P
FF = 2816
PAIRS = FF // 256
LAYERS = 2
RING = 3
UNIT = 2048
HALF = UNIT // 2
EPS = 1e-6
A_HEADS, A_DIM = 8, 64
B_HEADS, NOPE, ROPE, VDIM = 8, 64, 32, 64
Q_RANK, KV_RANK = 256, 128
QK_B = NOPE + ROPE
C_HEADS, C_DIM = 16, 64
AUG = 2
MLA_C = Q_RANK + KV_RANK + ROPE
HEADS = 16
BIG = 3.0e38

FFN_UNITS = 3 * PAIRS
AB1 = D
AB2 = 3 * A_HEADS * A_DIM + MLA_C - D
WIDTHS = []
START = {}


def _lay_out_units():
    def phase(name, widths):
        START[name] = len(WIDTHS)
        WIDTHS.extend(widths)
    for layer in range(LAYERS):
        phase(("ffn", 2 * layer), [UNIT] * FFN_UNITS)
        if layer == 0:
            phase("ab2", [2 * AB2] * 4)
            phase("ab1", [2 * AB1] * 4)
            phase("uq", [2 * B_HEADS * QK_B])
            phase("ukv", [B_HEADS * (NOPE + VDIM)])
        else:
            phase("fox_q", [UNIT] * 2)
            phase("fox_f", [KD * C_HEADS])
            phase("fox_q2", [UNIT] * 2)
            phase("fox_k", [UNIT] * 4)
            phase("fox_v", [UNIT] * 4)
        phase(("out", layer), [UNIT] * 4)
        phase(("ffn", 2 * layer + 1), [UNIT] * FFN_UNITS)
        phase(("gate", layer), [UNIT] * 4)
        phase(("proj", layer), [UNIT])


_lay_out_units()
N_UNITS = len(WIDTHS)


def program(nc, x_in, p_in, t5_bias, ff1_norm, ff1_w_in, ff1_w_out, mix_norm, ff2_norm, ff2_w_in,
            ff2_w_out, ple_norm, ple_w_gate, ple_w_proj, ab_w_in, mla_q_norm, mla_w_uq,
            mla_kv_norm, mla_w_ukv, ab_w_out, fox_w_in, fox_b_f, fox_w_out, final_norm,
            c_ident, c_upper, c_mask, c_cos, c_sin, c_onehot, c_future, out):
    f32, f32r = mybir.dt.float32, mybir.dt.float32r
    ACT = mybir.ActivationFunctionType
    AX = mybir.AxisListType

    ctx = ExitStack()
    with ctx:
        def sb(name, shape, dt=f32):
            return ctx.enter_context(nc.sbuf_tensor(name, shape, dt))

        def sem(name):
            return ctx.enter_context(nc.semaphore(name))

        raw = sb("raw", [P, RING, UNIT])
        w_hi = sb("w_hi", [P, RING, UNIT], f32r)
        w_lo = sb("w_lo", [P, RING, UNIT], f32r)
        x = sb("x", [P, T, D])
        xg = sb("xg", [P, T, D])
        h_hi = sb("h_hi", [P, KD, SEQ], f32r)
        h_lo = sb("h_lo", [P, KD, SEQ], f32r)
        act_a = sb("act_a", [P, 512])
        hid = sb("hid", [P, 512])
        hid_hi = sb("hid_hi", [P, 2, SEQ], f32r)
        hid_lo = sb("hid_lo", [P, 2, SEQ], f32r)
        gain = sb("gain", [P, 2, D])
        meansq = sb("meansq", [P, T])
        minus_half = sb("minus_half", [P, 2 * T])
        rstd = sb("rstd", [P, T])
        half_rstd = sb("half_rstd", [P, T])
        q_rstd = sb("q_rstd", [P, T])
        table = sb("table", [P, 1])
        junk = sb("junk", [P, D])
        diag = sb("diag", [P, T, P])
        rstd_row = sb("rstd_row", [P, SEQ])
        pT_hi = sb("pT_hi", [P, LAYERS, 2, SEQ], f32r)
        pT_lo = sb("pT_lo", [P, LAYERS, 2, SEQ], f32r)
        q_tok = sb("q_tok", [P, T, A_HEADS * A_DIM + B_HEADS * QK_B])
        k_tok = sb("k_tok", [P, T, D])
        v_tok = sb("v_tok", [P, T, D])
        comp = sb("comp", [P, T, MLA_C])
        comp_n = xg[:, :, 0:Q_RANK + KV_RANK]
        cT_hi = sb("cT_hi", [P, 3, SEQ], f32r)
        cT_lo = sb("cT_lo", [P, 3, SEQ], f32r)
        c_meansq = sb("c_meansq", [P, T, 2])
        c_rstd = sb("c_rstd", [P, T, 2])
        c_gain = sb("c_gain", [P, Q_RANK + KV_RANK])
        stage = sb("stage", [P, 2, 4, QK_B])
        qkT = sb("qkT", [P, 2, 512])
        neg_logits = sb("neg_logits", [P, 2, 384])
        neg_max = sb("neg_max", [P, 2, T])
        probs = sb("probs", [P, 2, 384])
        row_sum = sb("row_sum", [P, 2, T])
        row_inv = sb("row_inv", [P, 2, T])
        probsT = sb("probsT", [P, 2, 384])
        rope_t = sb("rope_t", [P, 4, B_HEADS, ROPE // 2])
        bias = sb("bias", [P, A_HEADS, 384])
        aug_q = sb("aug_q", [P, T, C_HEADS, AUG])
        aug_k = sb("aug_k", [P, T, C_HEADS, AUG])
        f_row = sb("f_row", [C_HEADS, SEQ])
        forget = sb("forget", [P, 5, T, C_HEADS])
        ident = sb("ident", [P, P])
        upper = sb("upper", [P, 2 * P])
        mask = sb("mask", [P, 384])
        cos = sb("cos", [P, T, ROPE // 2])
        sin = sb("sin", [P, T, ROPE // 2])
        t5_sb = sb("t5_sb", [32, A_HEADS])
        p_sb = k_tok[:, 1, :].rearrange("p (l t c) -> p l t c", l=LAYERS, t=T)
        t5_row, future, onehot = q_tok[0:A_HEADS, 0, 0:512], q_tok[0:A_HEADS, 0, 512:1024], k_tok[0:32, 0, 0:512]
        b_f = sb("b_f", [P, C_HEADS])
        t5_dram = nc.dram_tensor("t5_scratch", [A_HEADS, P, 512], f32, kind="Internal")

        bank = [ctx.enter_context(nc.psum_tensor(f"bank{i}", [P, 512], f32)) for i in range(8)]
        GATE, UP = bank[4], bank[5]

        raw_landed = [sem(f"raw_landed{s}") for s in range(RING)]
        half_landed = sem("half_landed")
        hi_split = sem("hi_split")
        lo_split = sem("lo_split")
        unit_used = sem("unit_used")
        x_landed = [sem("x_landed0"), sem("x_landed1")]
        ident_landed = sem("ident_landed")
        upper_landed = sem("upper_landed")
        half_gain_landed = sem("half_gain_landed")
        const_landed = sem("const_landed")
        t5_landed = sem("t5_landed")
        gain_landed = [sem("gain_landed0"), sem("gain_landed1")]
        x_ready = sem("x_ready")
        meansq_ready = sem("meansq_ready")
        rstd_ready = sem("rstd_ready")
        row_done = sem("row_done")
        row_copied = sem("row_copied")
        gate_scaled = sem("gate_scaled")
        root_step = sem("root_step")
        c_rstd_ready = sem("c_rstd_ready")
        xg_ready = sem("xg_ready")
        t_done = sem("t_done")
        h_hi_ready = sem("h_hi_ready")
        h_lo_ready = sem("h_lo_ready")
        y_part = sem("y_part")
        silu_done = sem("silu_done")
        hid_done = sem("hid_done")
        hid_hi_done = sem("hid_hi_done")
        hid_lo_done = sem("hid_lo_done")
        sig_done = sem("sig_done")
        gated = sem("gated")
        pT_done = sem("pT_done")
        pT_hi_done = sem("pT_hi_done")
        pT_lo_done = sem("pT_lo_done")
        t5_done = sem("t5_done")
        t5_row_done = sem("t5_row_done")
        t5_stored = sem("t5_stored")
        mix_act = sem("mix_act")
        mix_dve = sem("mix_dve")
        comp_sq = sem("comp_sq")
        comp_ready = sem("comp_ready")
        cT_done = sem("cT_done")
        cT_hi_done = sem("cT_hi_done")
        cT_lo_done = sem("cT_lo_done")
        rope_step = sem("rope_step")
        f_step = sem("f_step")
        table_loaded = sem("table_loaded")
        f_act = sem("f_act")
        fT_done = sem("fT_done")
        cum_done = sem("cum_done")
        aug_ready = sem("aug_ready")
        staged = sem("staged")
        qkT_done = sem("qkT_done")
        qkT_copied = sem("qkT_copied")
        logits_done = sem("logits_done")
        biased = sem("biased")
        max_done = sem("max_done")
        exp_done = sem("exp_done")
        probsT_done = sem("probsT_done")
        probsT_copied = sem("probsT_copied")
        inv_done = sem("inv_done")
        pv_done = sem("pv_done")
        head_done = sem("head_done")
        result_half = sem("result_half")
        out_stored = sem("out_stored")

        def Y0(t):
            return [bank[2 * t][:, :], bank[2 * t + 1][:, :]]

        def Z0(t):
            return [bank[4 + 2 * t][:, :], bank[5 + 2 * t][:, :]]

        FINAL = 4 * LAYERS
        CONSTS = 10
        F_Z, F_ABS, F_EXP, F_LN, F_LOG = range(5)
        F_STEPS = 4
        WARM_UP = 14
        ATTENTION_BANKS = ({"T": 4, "S": 6, "P": 2, "O": 0}, {"T": 2, "S": 0, "P": 6, "O": 4})

        def output_bank(h):
            layer, last_two = h // HEADS, h % HEADS >= HEADS - 2
            return (2 if layer and last_two else ATTENTION_BANKS[layer]["O"]) + h % 2

        PARTS = ((0, 0), (1, 0), (0, 1), (1, 1))

        def parts(b):
            return PARTS if b < FINAL else ((0, 0), (0, 1), (1, 0), (1, 1))

        norm_gain = []
        for layer in range(LAYERS):
            norm_gain += [ff1_norm[layer:layer + 1, :], mix_norm[layer:layer + 1, :],
                          ff2_norm[layer:layer + 1, :], ple_norm[layer:layer + 1, :]]
        norm_gain.append(final_norm.unsqueeze(0))

        def t_index(b):
            layer, k = divmod(b, 4)
            return 5 * layer + (k if k < 2 else k + 1)

        block = ctx.enter_context(nc.Block())

        @block.sync
        def _(sp):
            def load(n, source, i=0):
                if n >= RING:
                    sp.wait_ge(lo_split, 2 * (n - RING + 1) + 2 * RING * i)
                chunks = source.shape[1]
                sp.dma_start(raw[:, n % RING, 0:WIDTHS[n]].rearrange("p (k c) -> p k c", k=chunks),
                             source).then_inc(raw_landed[n % RING], 16)

            def rows(w, k0, nk, c0, width):
                return w[k0 * P:(k0 + nk) * P, c0:c0 + width].rearrange("(k p) c -> p k c", p=P)

            def load_x(c):
                for t in range(T):
                    cols = slice(c * 512, (c + 1) * 512)
                    sp.dma_start(x[:, t, cols], x_in[0, t * P:(t + 1) * P, cols]).then_inc(x_landed[c], 16)

            load_x(0)
            for layer in range(LAYERS):
                for half in range(2):
                    f = 2 * layer + half
                    w_in = (ff1_w_in, ff2_w_in)[half][layer, :, :].rearrange("(k p) c -> p k c", p=P)
                    w_out = (ff1_w_out, ff2_w_out)[half][layer, :, :].rearrange("(g p) c -> p g c", p=P)
                    n = START["ffn", f]

                    def gate_u(i):
                        return w_in[:, :, bass.ds(i * 256, 256)]

                    def up_u(i):
                        return w_in[:, :, bass.ds(i * 256 + FF, 256)]

                    def down_u(i):
                        return w_out[:, bass.ds(i * 2, 2), :]

                    if n == 0:
                        for j, landed in enumerate((half_landed, raw_landed[0])):
                            if j == 1:
                                load_x(1)
                            sp.dma_start(raw[:, 0, j * HALF:(j + 1) * HALF].rearrange("p (k c) -> p k c", k=KD // 2),
                                         w_in[:, j * KD // 2:(j + 1) * KD // 2, 0:256]).then_inc(landed, 16)
                    else:
                        load(n, gate_u(0))
                    load(n + 1, up_u(0))
                    load(n + 2, gate_u(1))
                    load(n + 3, down_u(0))
                    load(n + 4, up_u(1))
                    with sp.Fori(0, PAIRS - 3) as i:
                        load(n + 5, gate_u(i + 2), i)
                        load(n + 6, down_u(i + 1), i)
                        load(n + 7, up_u(i + 2), i)
                    load(n + 29, gate_u(PAIRS - 1))
                    load(n + 30, up_u(PAIRS - 1))
                    load(n + 31, down_u(PAIRS - 2))
                    load(n + 32, down_u(PAIRS - 1))
                    if half == 0 and layer == 0:
                        for j in range(4):
                            load(START["ab2"] + j, rows(ab_w_in[0], 2 * j, 2, AB1, AB2))
                        for j in range(4):
                            load(START["ab1"] + j, rows(ab_w_in[0], 2 * j, 2, 0, AB1))
                        load(START["uq"], rows(mla_w_uq[0], 0, 2, 0, B_HEADS * QK_B))
                        load(START["ukv"], rows(mla_w_ukv[0], 0, 1, 0, B_HEADS * (NOPE + VDIM)))
                    if half == 0 and layer == 1:
                        for j in range(2):
                            load(START["fox_q"] + j, rows(fox_w_in[0], 2 * j, 2, 0, D))
                        with nc.allow_non_contiguous_dma(reason="sixteen columns of gates"):
                            load(START["fox_f"], rows(fox_w_in[0], 0, KD, 3 * D, C_HEADS))
                        for j in range(2):
                            load(START["fox_q2"] + j, rows(fox_w_in[0], 4 + 2 * j, 2, 0, D))
                        for c, name in enumerate(("fox_k", "fox_v")):
                            for j in range(4):
                                load(START[name] + j, rows(fox_w_in[0], 2 * j, 2, (c + 1) * D, D))
                    if half == 0:
                        w = (ab_w_out, fox_w_out)[layer][0]
                        for j in range(4):
                            load(START["out", layer] + j, rows(w, 2 * j, 2, 0, D))
                for j in range(4):
                    load(START["gate", layer] + j, rows(ple_w_gate[layer], 2 * j, 2, 0, D))
                load(START["proj", layer], rows(ple_w_proj[layer], 0, 2, 0, D))
            for part, (t, c) in enumerate(parts(FINAL)):
                if part < 2:
                    sp.wait_ge(xg_ready, 4 * FINAL + part + 1)
                elif part == 2:
                    sp.wait_ge(result_half, 1)
                else:
                    sp.wait_ge(xg_ready, 4 * FINAL + 5)
                sp.dma_start(out[0, t * P:(t + 1) * P, c * 512:(c + 1) * 512],
                             xg[:, t, c * 512:(c + 1) * 512]).then_inc(out_stored, 16)
            sp.wait_ge(out_stored, 16 * 4)

        @block.gpsimd
        def _(pool):
            for c, landed in enumerate((half_gain_landed, gain_landed[0])):
                cols = slice(c * 512, (c + 1) * 512)
                pool.dma_start(gain[:, 0, cols], norm_gain[0][:, cols].partition_broadcast(P)).then_inc(landed, 16)
            pool.dma_start(upper[:, :], c_upper).then_inc(upper_landed, 16)
            pool.dma_start(p_sb, p_in.rearrange("l b (t q) c -> q (l b) t c", q=P)).then_inc(const_landed, 16)
            pool.dma_start(t5_sb[:, :], t5_bias).then_inc(const_landed, 16)
            pool.dma_start(onehot, c_onehot).then_inc(const_landed, 16)
            pool.dma_start(future, c_future).then_inc(const_landed, 16)
            pool.dma_start(mask[:, :], c_mask).then_inc(const_landed, 16)
            pool.dma_start(cos[:, :, :], c_cos.rearrange("(t p) c -> p t c", p=P)).then_inc(const_landed, 16)
            pool.dma_start(sin[:, :, :], c_sin.rearrange("(t p) c -> p t c", p=P)).then_inc(const_landed, 16)
            pool.dma_start(c_gain[:, 0:Q_RANK], mla_q_norm.partition_broadcast(P)).then_inc(const_landed, 16)
            pool.dma_start(c_gain[:, Q_RANK:], mla_kv_norm.partition_broadcast(P)).then_inc(const_landed, 16)
            pool.dma_start(b_f[:, :], fox_b_f.partition_broadcast(P)).then_inc(const_landed, 16)
            pool.dma_start(gain[:, 1, :], norm_gain[1].partition_broadcast(P)).then_inc(gain_landed[1], 16)

            def load_gain(b):
                pool.wait_ge(xg_ready, 4 * (b - 1))
                pool.dma_start(gain[:, b % 2, :], norm_gain[b].partition_broadcast(P)).then_inc(
                    gain_landed[b % 2], 16)

            roots = [0]

            def inverse_root(to, mean, exponent):
                nc.gpsimd.tensor_scalar(mean, mean, EPS, None, ALU.add).then_inc(root_step, 1)
                roots[0] += 1
                pool.wait_ge(root_step, roots[0])
                return nc.gpsimd.tensor_tensor(to, mean, exponent, ALU.pow)

            def rstds(b):
                for t in range(T):
                    pool.wait_ge(meansq_ready, T * b + t + 1)
                    last = inverse_root(rstd[:, t:t + 1], meansq[:, t:t + 1], minus_half[:, 0:1])
                    if b == FINAL:
                        last.then_inc(rstd_ready, 1)
                if b == FINAL:
                    return
                if b % 4 in (1, 3):
                    if b % 4 == 1:
                        last.then_inc(root_step, 1)
                        roots[0] += 1
                        pool.wait_ge(root_step, roots[0])
                        last = nc.gpsimd.tensor_scalar(q_rstd[:, :], rstd[:, :], -A_DIM ** -0.5, None, ALU.mult)
                    last.then_inc(rstd_ready, 1)
                else:
                    last.then_inc(root_step, 1)
                    roots[0] += 1
                    pool.wait_ge(root_step, roots[0])
                    nc.gpsimd.tensor_scalar(half_rstd[:, :], rstd[:, :], 0.5, None, ALU.mult)
                    if b == 0:
                        pool.wait_ge(ident_landed, 16)
                    for t in range(T):
                        last = nc.gpsimd.tensor_scalar(diag[:, t, :], ident[:, :], rstd[:, t:t + 1], None, ALU.mult)
                    last.then_inc(rstd_ready, 1)

            def stage_heads(first, start, end, kinds):
                def stage_head(h, s, used):
                    if used is not None:
                        pool.wait_ge(qkT_done, used)
                    for j, (block0, width, column, source) in enumerate(kinds):
                        ins = nc.gpsimd.tensor_copy(stage[:, s, block0:block0 + T, column:column + width],
                                                    source(h))
                    ins.then_inc(staged, 1)

                if end - start == 2:
                    for s in range(2):
                        stage_head(start + s, s, first + start + s - 1 if first + start else None)
                else:
                    with pool.Fori(0, (end - start) // 2) as i:
                        for s in range(2):
                            stage_head(i * 2 + (start + s), s, i * 2 + (first + start + s - 1))

            nc.gpsimd.memset(stage[:, :, :, :], 0.0).then_inc(root_step, 1)
            roots[0] += 1
            nc.gpsimd.memset(minus_half[:, :], -0.5).then_inc(root_step, 1)
            roots[0] += 1
            rstds(0)
            load_gain(2)
            rstds(1)
            load_gain(3)
            pool.wait_ge(t5_row_done, 1)
            pool.dma_start(t5_dram.ap(), t5_row.unsqueeze(1).to_broadcast([A_HEADS, P, 512])).then_inc(t5_stored, 16)
            pool.wait_ge(t5_stored, 16)
            for c0, c1, ahead in ((0, SEQ, 0), (SEQ, 384, P)):
                toeplitz = bass.AP(tensor=t5_dram, offset=P - 1 + ahead,
                                   ap=[[511, P], [P * 512, A_HEADS], [1, c1 - c0]])
                pool.dma_start(bias[:, :, c0:c1], toeplitz).then_inc(t5_landed, 16)
            half = ROPE // 2
            steps = [0]

            def rope_op(out_, a, b, op):
                nc.gpsimd.tensor_tensor(out_, a, b, op).then_inc(rope_step, 1)
                steps[0] += 1

            def rotate(x1, x2, co, si, tmp):
                if steps[0]:
                    pool.wait_ge(rope_step, steps[0])
                rope_op(tmp[0], x1, co, ALU.mult)
                rope_op(tmp[1], x2, si, ALU.mult)
                rope_op(tmp[2], x1, si, ALU.mult)
                rope_op(tmp[3], x2, co, ALU.mult)
                pool.wait_ge(rope_step, steps[0])
                rope_op(x1, tmp[0], tmp[1], ALU.subtract)
                rope_op(x2, tmp[2], tmp[3], ALU.add)

            pool.wait_ge(comp_sq, 4)
            inverse_root(c_rstd[:, :, :].rearrange("p t c -> p (t c)"),
                         c_meansq[:, :, :].rearrange("p t c -> p (t c)"), minus_half[:, :]).then_inc(c_rstd_ready, 1)
            pool.wait_ge(mix_dve, 1)
            pool.wait_ge(const_landed, 16 * CONSTS)
            rotate(comp[:, :, Q_RANK + KV_RANK:Q_RANK + KV_RANK + half],
                   comp[:, :, Q_RANK + KV_RANK + half:MLA_C], cos[:, :, :], sin[:, :, :],
                   [rope_t[:, j, 0:T, :] for j in range(4)])
            pool.wait_ge(mix_act, 2)
            pool.wait_ge(mix_dve, 2)
            moba = [(0, A_DIM, 0, lambda h: q_tok[:, :, bass.ds(h * A_DIM, A_DIM)]),
                    (2, A_DIM, 0, lambda h: k_tok[:, :, bass.ds(h * A_DIM, A_DIM)])]
            q_b = q_tok[:, :, A_HEADS * A_DIM:].rearrange("p t (h c) -> p t h c", h=B_HEADS)

            def rotate_q(t):
                wide = [P, B_HEADS, half]
                rotate(q_b[:, t, :, NOPE:NOPE + half], q_b[:, t, :, NOPE + half:QK_B],
                       cos[:, t:t + 1, :].to_broadcast(wide), sin[:, t:t + 1, :].to_broadcast(wide),
                       [rope_t[:, j, :, :] for j in range(4)])

            stage_heads(0, 0, 2, moba)
            pool.wait_ge(mix_act, 3)
            pool.wait_ge(mix_dve, 3)
            rotate_q(0)
            stage_heads(0, 2, A_HEADS - 2, moba)
            rotate_q(1)
            stage_heads(0, A_HEADS - 2, A_HEADS, moba)
            pool.wait_ge(mix_act, 4)
            pool.wait_ge(mix_dve, 4)
            pool.wait_ge(rope_step, steps[0])
            mla = [(0, QK_B, 0, lambda h: q_tok[:, :, bass.ds(h * QK_B + A_HEADS * A_DIM, QK_B)]),
                   (2, NOPE, 0, lambda h: k_tok[:, :, bass.ds(h * NOPE + A_HEADS * A_DIM, NOPE)]),
                   (2, ROPE, NOPE, lambda h: comp[:, :, Q_RANK + KV_RANK:MLA_C])]
            stage_heads(A_HEADS, 0, 2, mla)
            stage_heads(A_HEADS, 2, B_HEADS, mla)
            for b in range(2, 6):
                rstds(b)
                load_gain(b + 2)
            pool.wait_ge(aug_ready, 1)
            pool.wait_ge(mix_act, 6)
            pool.wait_ge(mix_dve, 6)
            fox = [(0, C_DIM, 0, lambda h: q_tok[:, :, bass.ds(h * C_DIM, C_DIM)]),
                   (2, C_DIM, 0, lambda h: k_tok[:, :, bass.ds(h * C_DIM, C_DIM)]),
                   (0, AUG, C_DIM, lambda h: aug_q[:, :, bass.ds(h, 1), :].rearrange("p t h c -> p t (h c)")),
                   (2, AUG, C_DIM, lambda h: aug_k[:, :, bass.ds(h, 1), :].rearrange("p t h c -> p t (h c)"))]
            stage_heads(HEADS, 0, 2, fox)
            stage_heads(HEADS, 2, C_HEADS, fox)
            for b in range(6, FINAL + 1):
                rstds(b)
                if b + 2 <= FINAL:
                    load_gain(b + 2)

        @block.tensor
        def _(pe):
            Y = [[bank[0], bank[1]], [bank[2], bank[3]]]
            Z = [[bank[4], bank[5]], [bank[6], bank[7]]]
            ROW = bank[7]

            def product(out_, a_hi, a_lo, b_hi, b_lo, start, stop):
                nc.tensor.matmul(out_, a_hi, b_hi, start=start, stop=False)
                nc.tensor.matmul(out_, a_hi, b_lo, start=False, stop=False)
                return nc.tensor.matmul(out_, a_lo, b_hi, start=False, stop=stop)

            def wide_unit(n, hi, lo, k0, banks, first, last, i=0):
                chunks = 1 if n == START["ukv"] else 2
                width = WIDTHS[n] // chunks
                s = n % RING
                pe.wait_ge(lo_split, i * (2 * RING) + 2 * (n + 1))
                for k in range(chunks):
                    for t in range(T):
                        for c in range((width + 511) // 512):
                            c0, c1 = k * width + 512 * c, k * width + min(512 * (c + 1), width)
                            ins = product(banks[t][c][:, 0:c1 - c0],
                                          hi[:, k0 + k, t * P:(t + 1) * P], lo[:, k0 + k, t * P:(t + 1) * P],
                                          w_hi[:, s, c0:c1], w_lo[:, s, c0:c1],
                                          start=first and k == 0, stop=last and k == chunks - 1)
                ins.then_inc(unit_used, 1)

            def transpose_part(source, part, banks):
                t, c = PARTS[part]
                for k in range(4):
                    ins = nc.tensor.transpose(banks[t][c][:, k * P:(k + 1) * P],
                                              source[:, t, c * 512 + k * P:c * 512 + (k + 1) * P], ident[:, :])
                ins.then_inc(t_done, 1)

            def closing_unit(n, hi, lo, k0, first, b):
                s, width = n % RING, WIDTHS[n] // 2
                pe.wait_ge(lo_split, 2 * (n + 1))
                for part, (t, c) in enumerate(parts(b)):
                    for k in range(2):
                        c0 = k * width + 512 * c
                        ins = product(Y[t][c][:, :], hi[:, k0 + k, t * P:(t + 1) * P],
                                      lo[:, k0 + k, t * P:(t + 1) * P],
                                      w_hi[:, s, c0:c0 + 512], w_lo[:, s, c0:c0 + 512],
                                      start=first and k == 0, stop=k == 1)
                    ins.then_inc(y_part if part < 3 else unit_used, 1)
                    if part and b < FINAL:
                        pe.wait_ge(xg_ready, 4 * b + part)
                        transpose_part(xg, part - 1, Y)

            def last_part(b):
                pe.wait_ge(xg_ready, 4 * b + 4)
                transpose_part(xg, 3, Y)

            def narrow_unit(n, target, i=0, b=None, chunks=range(KD)):
                s = n % RING
                hi = w_hi[:, s, :].rearrange("p (k c) -> p k c", k=KD)
                lo = w_lo[:, s, :].rearrange("p (k c) -> p k c", k=KD)
                for k in chunks:
                    if k == 0:
                        pe.wait_ge(lo_split, i * (2 * RING) + (2 * n + 1))
                    if k == KD // 2:
                        pe.wait_ge(lo_split, i * (2 * RING) + (2 * n + 2))
                    if b is not None and k == 0:
                        pe.wait_ge(h_lo_ready, 4 * t_index(b) + 2)
                    if b is not None and k == (2 if b else 1):
                        if b == 0:
                            pe.wait_ge(xg_ready, 3)
                            transpose_part(xg, 2, Y)
                        last_part(b)
                    if b is not None and k == KD // 2:
                        pe.wait_ge(h_lo_ready, 4 * t_index(b) + 4)
                    for g in range(2):
                        dst = target[:, g * SEQ:(g + 1) * SEQ]
                        w = slice(g * P, (g + 1) * P)
                        first, last = k == 0 and g == 0, k == KD - 1
                        nc.tensor.matmul(dst, hi[:, k, w], h_hi[:, k, :], start=first, stop=False,
                                         skip_group_check=True)
                        nc.tensor.matmul(dst, hi[:, k, w], h_lo[:, k, :], start=False, stop=False,
                                         skip_group_check=True)
                        ins = nc.tensor.matmul(dst, lo[:, k, w], h_hi[:, k, :], start=False, stop=last,
                                               skip_group_check=True)
                if k == KD - 1:
                    ins.then_inc(unit_used, 1)

            def ffn(f):
                n, p0 = START["ffn", f], PAIRS * f
                b = 4 * (f // 2) + 2 * (f % 2)

                def gate(n, pair, i=0, b=None, chunks=range(KD)):
                    if pair > 0:
                        pe.wait_ge(gate_scaled, i + pair)
                    narrow_unit(n, GATE, i, b, chunks)

                def up(n, pair, i=0, chunks=range(KD)):
                    if pair > 0:
                        pe.wait_ge(hid_done, i + pair)
                    narrow_unit(n, UP, i, None, chunks)

                def down(n, pair, i=0, first=False):
                    pe.wait_ge(hid_lo_done, i + (pair + 1))
                    wide_unit(n, hid_hi, hid_lo, 0, Y, first, False, i)

                if f:
                    gate(n, p0, 0, b, range(KD // 2))
                    up(n + 1, p0, 0, range(KD // 2))
                    gate(n, p0, 0, b, range(KD // 2, KD))
                else:
                    gate(n, p0, 0, b)
                    up(n + 1, p0, 0, range(KD // 2))
                pe.wait_ge(rstd_ready, b + 1)
                if f == 0:
                    pe.wait_ge(upper_landed, 16)
                for t in range(T):
                    ins = nc.tensor.matmul(ROW[:, t * P:(t + 1) * P], upper[:, 0:P], diag[:, t, :], start=True,
                                           stop=True)
                ins.then_inc(row_done, 1)
                up(n + 1, p0, 0, range(KD // 2, KD))
                if f == 0:
                    pe.wait_ge(const_landed, 16 * CONSTS)
                    transpose_embeddings(0, bank[6])
                gate(n + 2, p0 + 1)
                if f == 0:
                    pe.wait_ge(row_copied, 1)
                    transpose_embeddings(1, bank[7])
                down(n + 3, p0, first=True)
                if f == 0:
                    pe.wait_ge(pT_lo_done, 1)
                    nc.tensor.matmul(bank[6][0:A_HEADS, :], t5_sb[:, :], onehot, start=True,
                                     stop=True).then_inc(t5_done, 1)
                up(n + 4, p0 + 1)
                with pe.Fori(0, PAIRS - 3) as i:
                    gate(n + 5, p0 + 2, i)
                    down(n + 6, p0 + 1, i)
                    up(n + 7, p0 + 2, i)
                gate(n + 29, p0 + PAIRS - 1)
                up(n + 30, p0 + PAIRS - 1)
                down(n + 31, p0 + PAIRS - 2)
                pe.wait_ge(hid_lo_done, p0 + PAIRS)
                closing_unit(n + 32, cT_hi, cT_lo, 0, False, b + 1)

            def transpose_embeddings(layer, to):
                for k in range(2):
                    for t in range(T):
                        ins = nc.tensor.transpose(to[:, k * SEQ + t * P:k * SEQ + (t + 1) * P],
                                                  p_sb[:, layer, t, k * P:(k + 1) * P], ident[:, :])
                ins.then_inc(pT_done, 1)

            def project(name, banks, units=range(4), r=None, b=None):
                for j in units:
                    if r is not None and j in (0, 2):
                        pe.wait_ge(h_lo_ready, 4 * r + 2 + j)
                    wide_unit(START[name] + j, h_hi, h_lo, 2 * j, banks, j == 0, j == 3)
                    if b is not None and j == 0:
                        last_part(b)

            def transposes(h, s, at, banks):
                pe.wait_ge(staged, at(h + 1))
                if h >= 2:
                    pe.wait_ge(qkT_copied, at(h - 1))
                dt = QK_B if h < HEADS else C_DIM + AUG
                for j in range(4):
                    ins = nc.tensor.transpose(bank[banks["T"] + s][0:dt, j * P:(j + 1) * P],
                                              stage[:, s, j, 0:dt], ident[:, :])
                ins.then_inc(qkT_done, 1)

            def logits(h, s, at, banks, biased_before=1):
                d = A_DIM if h < A_HEADS else QK_B if h < HEADS else C_DIM + AUG
                lg = bank[banks["S"] + s]
                pe.wait_ge(qkT_copied, at(h + 1))
                if h >= 2:
                    pe.wait_ge(biased, at(h - biased_before))
                nc.tensor.matmul(lg[:, 0:SEQ], qkT[0:d, s, P:2 * P], qkT[0:d, s, 2 * P:4 * P],
                                 start=True, stop=True)
                nc.tensor.matmul(lg[:, SEQ:SEQ + P], qkT[0:d, s, 0:P], qkT[0:d, s, 2 * P:3 * P],
                                 start=True, stop=True).then_inc(logits_done, 1)

            def probabilities(h, s, at, banks):
                pe.wait_ge(exp_done, at(h + 1))
                for j in range(3):
                    ins = nc.tensor.transpose(bank[banks["P"] + s][:, j * P:(j + 1) * P],
                                              probs[:, s, j * P:(j + 1) * P], ident[:, :])
                ins.then_inc(probsT_done, 1)

            def values(h, s, at, banks, column):
                o = bank[output_bank(h)]
                pe.wait_ge(probsT_copied, at(h + 1))
                v = [v_tok[:, t, bass.ds(column, 64)] for t in range(T)]
                nc.tensor.matmul(o[:, 0:64], probsT[:, s, 2 * P:3 * P], v[0], start=True, stop=True)
                nc.tensor.matmul(o[:, 64:128], probsT[:, s, 0:P], v[0], start=True, stop=False)
                nc.tensor.matmul(o[:, 64:128], probsT[:, s, P:2 * P], v[1], start=False,
                                 stop=True).then_inc(pv_done, 1)

            def open_heads(first, banks):
                now = lambda v: v
                transposes(first, 0, now, banks)
                transposes(first + 1, 1, now, banks)
                logits(first, 0, now, banks)

            def open_more_heads(first, banks):
                now = lambda v: v
                transposes(first + 2, 0, now, banks)
                logits(first + 1, 1, now, banks)
                transposes(first + 3, 1, now, banks)

            def heads_in_loop(first, heads, banks):
                with pe.Fori(0, heads // 2) as i:
                    at = lambda v: i * 2 + v
                    for s in range(2):
                        h = first + s
                        probabilities(h, s, at, banks)
                        logits(h + 2, s, at, banks, 0)
                        transposes(h + 4, s, at, banks)
                        values(h, s, at, banks, i * 128 + h % HEADS * 64)

            def last_heads(first, end, banks):
                now = lambda v: v
                layer_end = -(-end // HEADS) * HEADS
                for h in range(first, end):
                    probabilities(h, h % 2, now, banks)
                    if h + 2 < layer_end:
                        logits(h + 2, h % 2, now, banks)
                    if h == layer_end - 2:
                        pe.wait_ge(head_done, h - 1)
                        transpose_part(xg, 0, Z)
                    if h == layer_end - 1:
                        transpose_part(xg, 1, Z)
                    if h + 4 < layer_end:
                        transposes(h + 4, h % 2, now, banks)
                    pe.wait_ge(head_done, h - 1)
                    values(h, h % 2, now, banks, h % HEADS * 64)

            pe.wait_ge(ident_landed, 16)
            for part in range(2):
                pe.wait_ge(xg_ready, part + 1)
                transpose_part(xg, part, Y)
            for _ in range(WARM_UP):
                nc.tensor.transpose(bank[7][:, 0:P], ident[:, :], ident[:, :])
            for layer in range(LAYERS):
                b = 4 * layer
                ffn(2 * layer)
                if layer == 0:
                    pe.wait_ge(pT_lo_done, 2)
                    pe.wait_ge(t5_row_done, 1)
                    project("ab2", Z, r=t_index(b + 1), b=b + 1)
                    project("ab1", Y, range(0, 2))
                    pe.wait_ge(mix_act, 1)
                    pe.wait_ge(mix_dve, 1)
                    for t in range(T):
                        pe.wait_ge(comp_ready, t + 1)
                        for k in range(3):
                            ins = nc.tensor.transpose(Z[t][0][:, k * P:(k + 1) * P],
                                                      comp_n[:, t, k * P:(k + 1) * P], ident[:, :])
                        ins.then_inc(cT_done, 1)
                    project("ab1", Y, range(2, 4))
                    pe.wait_ge(cT_lo_done, 2)
                    wide_unit(START["uq"], cT_hi, cT_lo, 0, Z, True, True)
                    pe.wait_ge(mix_act, 2)
                    pe.wait_ge(mix_dve, 2)
                    wide_unit(START["ukv"], cT_hi, cT_lo, 2, Y, True, True)
                    pe.wait_ge(mix_act, 3)
                    pe.wait_ge(mix_dve, 3)
                    banks = ATTENTION_BANKS[0]
                    open_heads(0, banks)
                    open_more_heads(0, banks)
                    pe.wait_ge(mix_act, 4)
                    pe.wait_ge(mix_dve, 4)
                    heads_in_loop(0, A_HEADS - 2, banks)
                    last_heads(A_HEADS - 2, A_HEADS, banks)
                    heads_in_loop(A_HEADS, B_HEADS - 4, banks)
                    last_heads(HEADS - 4, HEADS, banks)
                else:
                    r = t_index(b + 1)
                    project("fox_q", Z, range(0, 2), r=r, b=b + 1)
                    n, s = START["fox_f"], START["fox_f"] % RING
                    pe.wait_ge(lo_split, 2 * (n + 1))
                    pe.wait_ge(h_lo_ready, 4 * r + 4)
                    for k in range(KD):
                        cols = slice(k * C_HEADS, (k + 1) * C_HEADS)
                        ins = product(bank[0][0:C_HEADS, 0:SEQ], w_hi[:, s, cols], w_lo[:, s, cols],
                                      h_hi[:, k, :], h_lo[:, k, :], start=k == 0, stop=k == KD - 1)
                    ins.then_inc(unit_used, 1)
                    wide_unit(START["fox_q2"], h_hi, h_lo, 4, Z, False, False)
                    pe.wait_ge(f_step, 1)
                    for t in range(T):
                        ins = nc.tensor.transpose(bank[1][:, t * C_HEADS:(t + 1) * C_HEADS],
                                                  f_row[0:C_HEADS, t * P:(t + 1) * P],
                                                  ident[0:C_HEADS, 0:C_HEADS])
                    ins.then_inc(fT_done, 1)
                    wide_unit(START["fox_q2"] + 1, h_hi, h_lo, 6, Z, False, True)
                    pe.wait_ge(f_step, 2)
                    project("fox_k", Y, range(0, 3))
                    pe.wait_ge(mix_act, 5)
                    pe.wait_ge(mix_dve, 5)
                    pe.wait_ge(f_step, F_STEPS)
                    lf = forget[:, F_LOG, :, :]
                    nc.tensor.matmul(bank[4][:, 0:C_HEADS], upper[:, P:2 * P], lf[:, 0, :], start=True, stop=True)
                    nc.tensor.matmul(bank[4][:, C_HEADS:2 * C_HEADS], upper[:, 0:P], lf[:, 0, :], start=True,
                                     stop=False)
                    nc.tensor.matmul(bank[4][:, C_HEADS:2 * C_HEADS], upper[:, P:2 * P], lf[:, 1, :],
                                     start=False, stop=True).then_inc(cum_done, 1)
                    project("fox_k", Y, range(3, 4))
                    pe.wait_ge(aug_ready, 1)
                    project("fox_v", Z, range(0, 3))
                    pe.wait_ge(mix_act, 6)
                    pe.wait_ge(mix_dve, 6)
                    banks = ATTENTION_BANKS[1]
                    open_heads(HEADS, banks)
                    project("fox_v", Z, range(3, 4))
                    open_more_heads(HEADS, banks)
                    pe.wait_ge(mix_act, 7)
                    pe.wait_ge(mix_dve, 7)
                    heads_in_loop(HEADS, C_HEADS - 4, banks)
                    last_heads(2 * HEADS - 4, 2 * HEADS, banks)
                pe.wait_ge(head_done, HEADS * (layer + 1))
                transpose_part(xg, 2, Z)
                transpose_part(xg, 3, Z)
                r = 5 * layer + 2
                project(("out", layer), Y, range(0, 3), r)
                closing_unit(START["out", layer] + 3, h_hi, h_lo, 6, False, b + 2)
                ffn(2 * layer + 1)
                project(("gate", layer), Z, r=t_index(b + 3), b=b + 3)
                closing_unit(START["proj", layer], pT_hi[:, layer, :, :], pT_lo[:, layer, :, :], 0, True, b + 4)

        @block.scalar
        def _(act):
            def split(n, i=0):
                if n >= N_UNITS:
                    return
                s, half = n % RING, WIDTHS[n] // 2
                act.wait_ge(raw_landed[s], 16 * (n // RING + 1) + i * 16)
                if n >= RING:
                    act.wait_ge(unit_used, i * RING + (n - RING + 1))
                for j in range(2):
                    cols = slice(j * half, (j + 1) * half)
                    nc.scalar.copy(w_hi[:, s, cols], raw[:, s, cols]).then_inc(hi_split, 1)

            def splits_behind(name, count, first=0):
                for j in range(first, count):
                    split(START[name] + j + RING - 1)

            def mean_square(b, t):
                if b == 0:
                    act.wait_ge(x_landed[0], 16 * T)
                    act.wait_ge(x_landed[1], 16 * T)
                else:
                    act.wait_ge(x_ready, 4 * (b - 1) + (3 + t if b < FINAL else 2 + 2 * t))
                if b or t:
                    act.wait_ge(meansq_ready, T * b + t)
                nc.scalar.activation(junk[:, :], x[:, t, :], ACT.Square, scale=D ** -0.5,
                                     accum_out=meansq[:, t:t + 1]).then_inc(meansq_ready, 1)

            def input_hi(r, part, first_bank=0):
                act.wait_ge(t_done, 4 * r + part + 1)
                t, c = PARTS[part]
                nc.scalar.copy(h_hi[:, 4 * c:4 * c + 4, t * P:(t + 1) * P],
                               bank[first_bank + 2 * t + c][:, :].rearrange("p (k c) -> p k c", k=4)).then_inc(
                                   h_hi_ready, 1)

            def next_input(b, between=None):
                r = t_index(b)
                input_hi(r, 0)
                input_hi(r, 1)
                mean_square(b, 0)
                input_hi(r, 2)
                mean_square(b, 1)
                if between is not None:
                    split(between)
                input_hi(r, 3)

            def ffn(f):
                n, p0 = START["ffn", f], PAIRS * f

                def silu(pair, i=0):
                    act.wait_ge(gate_scaled, i + (pair + 1))
                    nc.scalar.activation(act_a[:, :], act_a[:, :], ACT.Silu).then_inc(silu_done, 1)

                def hidden_hi(pair, i=0, to=hid_hi):
                    act.wait_ge(hid_done, i + (pair + 1))
                    nc.scalar.copy(to[:, 0:2, :], hid[:, :].rearrange("p (g c) -> p g c", g=2)).then_inc(
                        hid_hi_done, 1)

                def embedding_hi(layer):
                    act.wait_ge(pT_done, layer + 1)
                    nc.scalar.copy(pT_hi[:, layer, :, :], bank[6 + layer][:, :].rearrange(
                        "p (k c) -> p k c", k=2)).then_inc(pT_hi_done, 1)

                split(n + 2)
                act.wait_ge(row_done, f + 1)
                nc.scalar.copy(rstd_row[:, :], bank[7][:, 0:SEQ]).then_inc(row_copied, 1)
                silu(p0)
                split(n + 3)
                hidden_hi(p0)
                if f == 0:
                    embedding_hi(0)
                split(n + 4)
                silu(p0 + 1)
                if f == 0:
                    embedding_hi(1)
                split(n + 5)
                split(n + 6)
                hidden_hi(p0 + 1)
                with act.Fori(0, PAIRS - 3) as i:
                    split(n + 7, i)
                    silu(p0 + 2, i)
                    split(n + 8, i)
                    split(n + 9, i)
                    hidden_hi(p0 + 2, i)
                split(n + 31)
                silu(p0 + PAIRS - 1)
                split(n + 32)
                hidden_hi(p0 + PAIRS - 1, 0, cT_hi)
                split(n + 33)
                split(n + 34)

            def copy_qkT(h, s, at):
                act.wait_ge(qkT_done, at(h + 1))
                if h >= 2:
                    act.wait_ge(logits_done, at(h - 1))
                d = QK_B if h < HEADS else C_DIM + AUG
                nc.scalar.copy(qkT[0:d, s, :],
                               bank[ATTENTION_BANKS[h // HEADS]["T"] + s][0:d, :]).then_inc(qkT_copied, 1)

            def exps(h, s, at):
                act.wait_ge(max_done, at(h + 1))
                nc.scalar.activation(probs[:, s, 0:SEQ], neg_logits[:, s, 0:SEQ], ACT.Exp, scale=-1.0,
                                     bias=neg_max[:, s, 1:2], accum_out=row_sum[:, s, 1:2])
                nc.scalar.activation(probs[:, s, SEQ:], neg_logits[:, s, SEQ:], ACT.Exp, scale=-1.0,
                                     bias=neg_max[:, s, 0:1], accum_out=row_sum[:, s, 0:1]).then_inc(exp_done, 1)

            def copy_probsT(h, s, at):
                act.wait_ge(probsT_done, at(h + 1))
                nc.scalar.copy(probsT[:, s, :],
                               bank[ATTENTION_BANKS[h // HEADS]["P"] + s][:, 0:384]).then_inc(probsT_copied, 1)

            def open_heads(first, end):
                for h in range(first, end):
                    copy_qkT(h, h % 2, lambda v: v)

            def heads_in_loop(first, heads):
                with act.Fori(0, heads // 2) as i:
                    for s in range(2):
                        copy_probsT(first + s, s, lambda v: i * 2 + v)
                        exps(first + 1 + s, 1 - s, lambda v: i * 2 + v)
                        copy_qkT(first + 4 + s, s, lambda v: i * 2 + v)

            def last_heads(first, end):
                layer_end = -(-end // HEADS) * HEADS
                for h in range(first, end):
                    copy_probsT(h, h % 2, lambda v: v)
                    if h + 1 < layer_end:
                        exps(h + 1, (h + 1) % 2, lambda v: v)
                    if h + 4 < layer_end:
                        copy_qkT(h + 4, h % 2, lambda v: v)

            tables = [0]

            def load_table(function):
                if tables[0]:
                    act.wait_ge(table_loaded, tables[0])
                nc.scalar.activation(table[:, :], minus_half[:, 0:1], function).then_inc(table_loaded, 1)
                tables[0] += 1

            act.dma_start(ident[:, :], c_ident).then_inc(ident_landed, 16)
            def split_first(half, landed):
                act.wait_ge(landed, 16)
                cols = slice(half * HALF, (half + 1) * HALF)
                nc.scalar.copy(w_hi[:, 0, cols], raw[:, 0, cols]).then_inc(hi_split, 1)

            input_hi(0, 0)
            input_hi(0, 1)
            split_first(0, half_landed)
            mean_square(0, 0)
            split_first(1, raw_landed[0])
            mean_square(0, 1)
            input_hi(0, 2)
            input_hi(0, 3)
            split(1)
            for layer in range(LAYERS):
                b = 4 * layer
                ffn(2 * layer)
                next_input(b + 1, START["ffn", 2 * layer] + FFN_UNITS + RING - 1)
                if layer == 0:
                    splits_behind("ab2", 4, 1)
                    act.wait_ge(rstd_ready, b + 2)
                    act.wait_ge(unit_used, START["ab2"] + 4)
                    for t in range(T):
                        ins = nc.scalar.mul(v_tok[:, t, 0:512], Z0(t)[0], rstd[:, t:t + 1])
                    ins.then_inc(mix_act, 1)
                    act.wait_ge(mix_dve, 1)
                    for t in range(T):
                        for j, (c0, c1) in enumerate(((0, Q_RANK), (Q_RANK, Q_RANK + KV_RANK))):
                            ins = nc.scalar.activation(comp_n[:, t, c0:c1], comp[:, t, c0:c1], ACT.Square,
                                                       scale=(c1 - c0) ** -0.5,
                                                       accum_out=c_meansq[:, t, j:j + 1])
                            ins.then_inc(comp_sq, 1)
                    splits_behind("ab1", 2)
                    for t in range(T):
                        act.wait_ge(cT_done, t + 1)
                        nc.scalar.copy(cT_hi[:, :, t * P:(t + 1) * P],
                                       Z0(t)[0][:, 0:3 * P].rearrange("p (k c) -> p k c", k=3)).then_inc(
                                           cT_hi_done, 1)
                    splits_behind("ab1", 4, 2)
                    load_table(ACT.Exp)
                    act.wait_ge(unit_used, START["ab1"] + 4)
                    act.wait_ge(t5_stored, 16)
                    for t in range(T):
                        ins = nc.scalar.mul(q_tok[:, t, 0:512], Y0(t)[0], q_rstd[:, t:t + 1])
                    ins.then_inc(mix_act, 1)
                    splits_behind("uq", 1)
                    act.wait_ge(unit_used, START["uq"] + 1)
                    for t in range(T):
                        ins = nc.scalar.mul(q_tok[:, t, 512:1024], Z0(t)[0], -QK_B ** -0.5)
                    ins.then_inc(mix_act, 1)
                    open_heads(0, 2)
                    act.wait_ge(unit_used, START["ukv"] + 1)
                    for t in range(T):
                        kv = Y0(t)[0].rearrange("p (h c) -> p h c", h=4)
                        nc.scalar.copy(k_tok[:, t, 512:768].rearrange("p (h c) -> p h c", h=4), kv[:, :, 0:NOPE])
                        ins = nc.scalar.copy(v_tok[:, t, 512:768].rearrange("p (h c) -> p h c", h=4),
                                             kv[:, :, NOPE:])
                    ins.then_inc(mix_act, 1)
                    open_heads(2, 3)
                    exps(0, 0, lambda v: v)
                    open_heads(3, 4)
                    heads_in_loop(0, HEADS - 4)
                    last_heads(HEADS - 4, HEADS)
                else:
                    splits_behind("fox_q", 2, 1)
                    splits_behind("fox_f", 1)
                    splits_behind("fox_q2", 2)
                    act.wait_ge(rstd_ready, b + 2)
                    act.wait_ge(unit_used, START["fox_q2"] + 2)
                    for t in range(T):
                        ins = nc.scalar.mul(q_tok[:, t, 0:512], Z0(t)[0], q_rstd[:, t:t + 1])
                    ins.then_inc(mix_act, 1)
                    splits_behind("fox_k", 1)
                    act.wait_ge(f_step, 3)
                    nc.scalar.activation(forget[:, F_EXP, :, :], forget[:, F_ABS, :, :], ACT.Exp,
                                         scale=-1.0).then_inc(f_act, 1)
                    splits_behind("fox_k", 2, 1)
                    act.wait_ge(f_act, 1)
                    nc.scalar.activation(forget[:, F_LN, :, :], forget[:, F_EXP, :, :], ACT.Ln,
                                         bias=1.0).then_inc(f_act, 1)
                    splits_behind("fox_k", 4, 2)
                    act.wait_ge(unit_used, START["fox_k"] + 4)
                    for t in range(T):
                        ins = nc.scalar.mul(k_tok[:, t, 0:512], Y0(t)[0], rstd[:, t:t + 1])
                    ins.then_inc(mix_act, 1)
                    load_table(ACT.Exp)
                    splits_behind("fox_v", 3)
                    open_heads(HEADS, HEADS + 2)
                    exps(HEADS, 0, lambda v: v)
                    act.wait_ge(unit_used, START["fox_v"] + 4)
                    for t in range(T):
                        ins = nc.scalar.mul(v_tok[:, t, 0:512], Z0(t)[0], rstd[:, t:t + 1])
                    ins.then_inc(mix_act, 1)
                    open_heads(HEADS + 2, HEADS + 4)
                    heads_in_loop(HEADS, HEADS - 4)
                    last_heads(2 * HEADS - 4, 2 * HEADS)
                for part in range(4):
                    input_hi(5 * layer + 2, part, 4)
                split(START["out", layer] + 1)
                splits_behind(("out", layer), 4)
                next_input(b + 2)
                ffn(2 * layer + 1)
                next_input(b + 3, START["gate", layer] + RING - 1)
                load_table(ACT.Sigmoid)
                splits_behind(("gate", layer), 4, 1)
                act.wait_ge(rstd_ready, b + 4)
                act.wait_ge(unit_used, START["gate", layer] + 4)
                for t, c in parts(b + 4):
                    nc.scalar.activation(xg[:, t, 512 * c:512 * (c + 1)], Z0(t)[c],
                                         ACT.Sigmoid, scale=rstd[:, t:t + 1]).then_inc(sig_done, 1)
                splits_behind(("proj", layer), 1)
                if layer + 1 < LAYERS:
                    next_input(b + 4)
            mean_square(FINAL, 0)
            mean_square(FINAL, 1)
            act.wait_ge(rstd_ready, FINAL + 2)
            act.wait_ge(xg_ready, 4 * FINAL + 3)
            nc.scalar.mul(xg[:, 1, 0:512], xg[:, 1, 0:512], rstd[:, 1:2]).then_inc(result_half, 1)

        @block.vector
        def _(dve):
            def split(n, i=0, halves=(0, 1)):
                if n >= N_UNITS:
                    return
                s, half = n % RING, WIDTHS[n] // 2
                for j in halves:
                    dve.wait_ge(hi_split, i * (2 * RING) + (2 * n + j + 1))
                    cols = slice(j * half, (j + 1) * half)
                    nc.vector.tensor_tensor(w_lo[:, s, cols], raw[:, s, cols], w_hi[:, s, cols].bitcast(f32),
                                            ALU.subtract).then_inc(lo_split, 1)

            def splits_behind(name, count, first=0):
                for j in range(first, count):
                    split(START[name] + j + RING - 1)

            def times_gain(b, part):
                t, c = parts(b)[part]
                cols = slice(512 * c, 512 * (c + 1))
                nc.vector.tensor_tensor(xg[:, t, cols], x[:, t, cols], gain[:, b % 2, cols],
                                        ALU.mult).then_inc(xg_ready, 1)

            def input_lo(r, part, first_bank=0):
                dve.wait_ge(h_hi_ready, 4 * r + part + 1)
                t, c = PARTS[part]
                to = slice(4 * c, 4 * c + 4), slice(t * P, (t + 1) * P)
                nc.vector.tensor_tensor(h_lo[:, to[0], to[1]],
                                        bank[first_bank + 2 * t + c][:, :].rearrange("p (k c) -> p k c", k=4),
                                        h_hi[:, to[0], to[1]].bitcast(f32), ALU.subtract).then_inc(h_lo_ready, 1)

            sums = [0]

            def next_input(b, closing, factor, between=None):
                for part, (t, c) in enumerate(parts(b)):
                    cols = slice(512 * c, 512 * (c + 1))
                    if factor is None:
                        dve.wait_ge(sig_done, 4 * (b // 4 - 1) + part + 1)
                    if part < 3:
                        sums[0] += 1
                        dve.wait_ge(y_part, sums[0])
                    else:
                        dve.wait_ge(unit_used, closing + 1)
                    if factor is None:
                        nc.vector.tensor_tensor(xg[:, t, cols], xg[:, t, cols], bank[2 * t + c][:, :],
                                                ALU.mult).then_inc(gated, 1)
                        dve.wait_ge(gated, 4 * (b // 4 - 1) + part + 1)
                        nc.vector.tensor_tensor(x[:, t, cols], x[:, t, cols], xg[:, t, cols],
                                                ALU.add).then_inc(x_ready, 1)
                    else:
                        nc.vector.scalar_tensor_tensor(x[:, t, cols], bank[2 * t + c][:, :], factor(t),
                                                       x[:, t, cols], ALU.mult, ALU.add).then_inc(x_ready, 1)
                    if b < FINAL:
                        dve.wait_ge(x_ready, 4 * (b - 1) + part + 1)
                        if part == 0:
                            dve.wait_ge(gain_landed[b % 2], 16 * (b // 2 + 1))
                        times_gain(b, part)
                        if part:
                            input_lo(t_index(b), part - 1)
                if between is not None:
                    split(between[0], 0, between[1])
                if b < FINAL:
                    input_lo(t_index(b), 3)

            def ffn(f):
                n, p0 = START["ffn", f], PAIRS * f
                b = 4 * (f // 2) + 2 * (f % 2)

                def scale_gate(n, pair, i=0):
                    dve.wait_ge(unit_used, i * RING + (n + 1))
                    nc.vector.tensor_tensor(act_a[:, :].rearrange("p (g c) -> p g c", g=2),
                                            GATE[:, :].rearrange("p (g c) -> p g c", g=2),
                                            rstd_row[:, :].unsqueeze(1).to_broadcast([P, 2, SEQ]),
                                            ALU.mult).then_inc(gate_scaled, 1)

                def hidden(n, pair, i=0, hi=hid_hi, lo=hid_lo):
                    dve.wait_ge(silu_done, i + (pair + 1))
                    dve.wait_ge(unit_used, i * RING + (n + 1))
                    nc.vector.tensor_tensor(hid[:, :], act_a[:, :], UP[:, :], ALU.mult).then_inc(hid_done, 1)
                    dve.wait_ge(hid_hi_done, i + (pair + 1))
                    nc.vector.tensor_tensor(lo[:, 0:2, :], hid[:, :].rearrange("p (g c) -> p g c", g=2),
                                            hi[:, 0:2, :].bitcast(f32), ALU.subtract).then_inc(hid_lo_done, 1)

                def embedding_lo(layer):
                    dve.wait_ge(pT_hi_done, layer + 1)
                    nc.vector.tensor_tensor(pT_lo[:, layer, :, :],
                                            bank[6 + layer][:, :].rearrange("p (k c) -> p k c", k=2),
                                            pT_hi[:, layer, :, :].bitcast(f32), ALU.subtract).then_inc(pT_lo_done, 1)

                split(n + 2)
                dve.wait_ge(row_copied, f + 1)
                scale_gate(n, p0)
                split(n + 3)
                hidden(n + 1, p0)
                if f == 0:
                    embedding_lo(0)
                split(n + 4)
                scale_gate(n + 2, p0 + 1)
                if f == 0:
                    embedding_lo(1)
                split(n + 5)
                if f == 0:
                    dve.wait_ge(const_landed, 16 * CONSTS)
                    dve.wait_ge(t5_done, 1)
                    nc.vector.tensor_tensor(t5_row, future, bank[6][0:A_HEADS, :], ALU.add).then_inc(t5_row_done, 1)
                split(n + 6)
                hidden(n + 4, p0 + 1)
                with dve.Fori(0, PAIRS - 3) as i:
                    split(n + 7, i)
                    scale_gate(n + 5, p0 + 2, i)
                    split(n + 8, i)
                    split(n + 9, i)
                    hidden(n + 7, p0 + 2, i)
                split(n + 31)
                scale_gate(n + 29, p0 + PAIRS - 1)
                split(n + 32)
                hidden(n + 30, p0 + PAIRS - 1, 0, cT_hi, cT_lo)
                split(n + 33)
                next_input(b + 1, n + 32, lambda t: half_rstd[:, t:t + 1], (n + 34, (0, 1)))

            def maxima(h, s, at, head):
                dve.wait_ge(logits_done, at(h + 1))
                if h >= 2:
                    dve.wait_ge(exp_done, at(h - 1))
                negated_bias = (bias[:, bass.ds(head, 1), :].rearrange("p h c -> p (h c)") if h < A_HEADS
                                else mask[:, :])
                nc.vector.tensor_tensor(neg_logits[:, s, :], negated_bias,
                                        bank[ATTENTION_BANKS[h // HEADS]["S"] + s][:, 0:384],
                                        ALU.add).then_inc(biased, 1)
                dve.wait_ge(biased, at(h + 1))
                nc.vector.tensor_reduce(neg_max[:, s, 1:2], neg_logits[:, s, 0:SEQ], AX.X, ALU.min)
                nc.vector.tensor_reduce(neg_max[:, s, 0:1], neg_logits[:, s, SEQ:], AX.X,
                                        ALU.min).then_inc(max_done, 1)

            def invert(h, s, at):
                dve.wait_ge(exp_done, at(h + 1))
                nc.vector.reciprocal(row_inv[:, s, :], row_sum[:, s, :]).then_inc(inv_done, 1)

            def output(h, s, at, column):
                dve.wait_ge(pv_done, at(h + 1))
                dve.wait_ge(inv_done, at(h + 1))
                nc.vector.tensor_tensor(xg[:, :, bass.ds(column, 64)],
                                        bank[output_bank(h)][:, 0:P].rearrange(
                                            "p (t c) -> p t c", t=T),
                                        row_inv[:, s, :].unsqueeze(2).to_broadcast([P, T, 64]),
                                        ALU.mult).then_inc(head_done, 1)

            def heads_in_loop(first, heads):
                with dve.Fori(0, heads // 2) as i:
                    for s in range(2):
                        at = lambda v: i * 2 + v
                        invert(first + s, s, at)
                        maxima(first + 2 + s, s, at, i * 2 + (2 + s))
                        output(first + s, s, at, i * 128 + (first + s) % HEADS * 64)

            def last_heads(first, end):
                for h in range(first, end):
                    invert(h, h % 2, lambda v: v)
                    if h + 2 < -(-end // HEADS) * HEADS:
                        maxima(h + 2, h % 2, lambda v: v, h + 2)
                    output(h, h % 2, lambda v: v, h % HEADS * 64)

            dve.wait_ge(half_gain_landed, 16)
            dve.wait_ge(x_landed[0], 16 * T)
            times_gain(0, 0)
            times_gain(0, 1)
            input_lo(0, 0)
            input_lo(0, 1)
            split(0, 0, (0,))
            dve.wait_ge(gain_landed[0], 16)
            dve.wait_ge(x_landed[1], 16 * T)
            times_gain(0, 2)
            times_gain(0, 3)
            split(0, 0, (1,))
            input_lo(0, 2)
            input_lo(0, 3)
            split(1)
            for layer in range(LAYERS):
                b = 4 * layer
                ffn(2 * layer)
                if layer == 0:
                    splits_behind("ab2", 4)
                    dve.wait_ge(rstd_ready, b + 2)
                    dve.wait_ge(unit_used, START["ab2"] + 4)
                    for t in range(T):
                        ins = nc.vector.tensor_scalar(comp[:, t, :], Z0(t)[1][:, 0:MLA_C], rstd[:, t:t + 1], None,
                                                      ALU.mult)
                    ins.then_inc(mix_dve, 1)
                    splits_behind("ab1", 1)
                    dve.wait_ge(c_rstd_ready, 1)
                    for t in range(T):
                        for j, (c0, c1) in enumerate(((0, Q_RANK), (Q_RANK, Q_RANK + KV_RANK))):
                            ins = nc.vector.scalar_tensor_tensor(comp_n[:, t, c0:c1], comp[:, t, c0:c1],
                                                                 c_rstd[:, t, j:j + 1], c_gain[:, c0:c1],
                                                                 ALU.mult, ALU.mult)
                        ins.then_inc(comp_ready, 1)
                    splits_behind("ab1", 2, 1)
                    for t in range(T):
                        dve.wait_ge(cT_hi_done, t + 1)
                        nc.vector.tensor_tensor(cT_lo[:, :, t * P:(t + 1) * P],
                                                Z0(t)[0][:, 0:3 * P].rearrange("p (k c) -> p k c", k=3),
                                                cT_hi[:, :, t * P:(t + 1) * P].bitcast(f32),
                                                ALU.subtract).then_inc(cT_lo_done, 1)
                    splits_behind("ab1", 4, 2)
                    dve.wait_ge(unit_used, START["ab1"] + 4)
                    for t in range(T):
                        ins = nc.vector.tensor_scalar(k_tok[:, t, 0:512], Y0(t)[1], rstd[:, t:t + 1], None, ALU.mult)
                    ins.then_inc(mix_dve, 1)
                    splits_behind("uq", 1)
                    dve.wait_ge(unit_used, START["uq"] + 1)
                    for t in range(T):
                        ins = nc.vector.tensor_scalar(q_tok[:, t, 1024:1280], Z0(t)[1][:, 0:256],
                                                      -QK_B ** -0.5, None, ALU.mult)
                    ins.then_inc(mix_dve, 1)
                    dve.wait_ge(unit_used, START["ukv"] + 1)
                    for t in range(T):
                        kv = Y0(t)[1].rearrange("p (h c) -> p h c", h=4)
                        nc.vector.tensor_copy(k_tok[:, t, 768:1024].rearrange("p (h c) -> p h c", h=4),
                                              kv[:, :, 0:NOPE])
                        ins = nc.vector.tensor_copy(v_tok[:, t, 768:1024].rearrange("p (h c) -> p h c", h=4),
                                                    kv[:, :, NOPE:])
                    ins.then_inc(mix_dve, 1)
                    dve.wait_ge(t5_landed, 32)
                    maxima(0, 0, lambda v: v, 0)
                    maxima(1, 1, lambda v: v, 1)
                    heads_in_loop(0, A_HEADS - 2)
                    last_heads(A_HEADS - 2, A_HEADS)
                    heads_in_loop(A_HEADS, B_HEADS - 4)
                    last_heads(HEADS - 4, HEADS)
                else:
                    splits_behind("fox_q", 2)
                    dve.wait_ge(unit_used, START["fox_f"] + 1)
                    nc.vector.tensor_copy(f_row[:, :], bank[0][0:C_HEADS, 0:SEQ]).then_inc(f_step, 1)
                    splits_behind("fox_f", 1)
                    splits_behind("fox_q2", 1)
                    dve.wait_ge(rstd_ready, b + 2)
                    dve.wait_ge(fT_done, 1)
                    z = forget[:, F_Z, :, :]
                    for t in range(T):
                        ins = nc.vector.scalar_tensor_tensor(z[:, t, :], bank[1][:, t * C_HEADS:(t + 1) * C_HEADS],
                                                             rstd[:, t:t + 1], b_f[:, :], ALU.mult, ALU.add)
                    ins.then_inc(f_step, 1)
                    dve.wait_ge(f_step, 2)
                    nc.vector.scalar_tensor_tensor(forget[:, F_ABS, :, :], z, -1.0, z, ALU.mult,
                                                   ALU.max).then_inc(f_step, 1)
                    splits_behind("fox_q2", 2, 1)
                    dve.wait_ge(unit_used, START["fox_q2"] + 2)
                    for t in range(T):
                        ins = nc.vector.tensor_scalar(q_tok[:, t, 512:1024], Z0(t)[1], q_rstd[:, t:t + 1], None,
                                                      ALU.mult)
                    ins.then_inc(mix_dve, 1)
                    splits_behind("fox_k", 2)
                    dve.wait_ge(f_act, 2)
                    nc.vector.scalar_tensor_tensor(forget[:, F_LOG, :, :], z, 0.0, forget[:, F_LN, :, :],
                                                   ALU.min, ALU.subtract).then_inc(f_step, 1)
                    splits_behind("fox_k", 3, 2)
                    dve.wait_ge(cum_done, 1)
                    cum = bank[4][:, 0:T * C_HEADS].rearrange("p (t h) -> p t h", t=T)
                    nc.vector.memset(aug_q[:, :, :, 0], -1.0)
                    nc.vector.memset(aug_k[:, :, :, 1], 1.0)
                    nc.vector.tensor_scalar(aug_q[:, :, :, 1], cum, -1.0, None, ALU.mult)
                    nc.vector.tensor_scalar(aug_k[:, :, :, 0], cum, -1.0, None, ALU.mult).then_inc(aug_ready, 1)
                    splits_behind("fox_k", 4, 3)
                    dve.wait_ge(unit_used, START["fox_k"] + 4)
                    for t in range(T):
                        ins = nc.vector.tensor_scalar(k_tok[:, t, 512:1024], Y0(t)[1], rstd[:, t:t + 1], None,
                                                      ALU.mult)
                    ins.then_inc(mix_dve, 1)
                    splits_behind("fox_v", 3)
                    maxima(HEADS, 0, lambda v: v, 0)
                    dve.wait_ge(unit_used, START["fox_v"] + 4)
                    for t in range(T):
                        ins = nc.vector.tensor_scalar(v_tok[:, t, 512:1024], Z0(t)[1], rstd[:, t:t + 1], None,
                                                      ALU.mult)
                    ins.then_inc(mix_dve, 1)
                    maxima(HEADS + 1, 1, lambda v: v, 1)
                    heads_in_loop(HEADS, HEADS - 4)
                    last_heads(2 * HEADS - 4, 2 * HEADS)
                for part in range(4):
                    input_lo(5 * layer + 2, part, 4)
                split(START["out", layer] + 1)
                up0 = START["ffn", 2 * layer + 1] + 1
                splits_behind(("out", layer), 3)
                next_input(b + 2, START["out", layer] + 3, lambda t: 1.0, (up0, (0,)))
                split(up0, 0, (1,))
                ffn(2 * layer + 1)
                splits_behind(("gate", layer), 4)
                if layer + 1 < LAYERS:
                    up0 = START["ffn", 2 * layer + 2] + 1
                    next_input(b + 4, START["proj", layer], None, (up0, (0,)))
                    split(up0, 0, (1,))
                else:
                    next_input(b + 4, START["proj", layer], None)
            dve.wait_ge(gain_landed[FINAL % 2], 16 * (FINAL // 2 + 1))
            for c in range(2):
                dve.wait_ge(rstd_ready, FINAL + 1)
                cols = slice(512 * c, 512 * (c + 1))
                nc.vector.scalar_tensor_tensor(xg[:, 0, cols], x[:, 0, cols], rstd[:, 0:1],
                                               gain[:, FINAL % 2, cols], ALU.mult, ALU.mult).then_inc(xg_ready, 1)
            dve.wait_ge(x_ready, 4 * FINAL)
            for part in (2, 3):
                times_gain(FINAL, part)
            dve.wait_ge(rstd_ready, FINAL + 2)
            dve.wait_ge(xg_ready, 4 * FINAL + 4)
            nc.vector.tensor_scalar(xg[:, 1, 512:1024], xg[:, 1, 512:1024], rstd[:, 1:2], None,
                                    ALU.mult).then_inc(xg_ready, 1)


_INS = ["x", "p", "t5_bias", "ff1_norm", "ff1_w_in", "ff1_w_out", "mix_norm", "ff2_norm", "ff2_w_in",
        "ff2_w_out", "ple_norm", "ple_w_gate", "ple_w_proj", "ab_w_in", "mla_q_norm", "mla_w_uq",
        "mla_kv_norm", "mla_w_ukv", "ab_w_out", "fox_w_in", "fox_b_f", "fox_w_out", "final_norm"]


def constants():
    import math
    import numpy as np
    f = np.float32
    token = np.arange(P)
    upper = np.concatenate([np.ones((P, P), f), (token[:, None] <= token[None, :]).astype(f)], 1)
    triangle = np.where(token[None, :] > token[:, None], f(1e30), f(0))
    mask = np.concatenate([np.zeros((P, P), f), triangle, triangle], 1)
    half = ROPE // 2
    inv = (f(10000.0) ** (-np.arange(half, dtype=f) / f(half))).astype(f)
    angle = np.arange(SEQ, dtype=f)[:, None] * inv[None, :]
    dist = SEQ - 1 - np.arange(512)
    d = np.maximum(dist.astype(f), f(1.0))
    large = 16 + (np.log(d / f(16)) / f(math.log(128 / 16)) * f(16)).astype(np.int32)
    bucket = np.where(dist < 16, np.maximum(dist, 0), np.minimum(large, 31))
    onehot = -(np.arange(32)[:, None] == bucket[None, :]).astype(f)
    future = np.broadcast_to(np.where(dist < 0, f(1e30), f(0)), (A_HEADS, 512))
    return {"c_ident": np.eye(P, dtype=f), "c_upper": upper, "c_mask": mask.astype(f),
            "c_cos": np.cos(angle).astype(f), "c_sin": np.sin(angle).astype(f),
            "c_onehot": onehot, "c_future": np.ascontiguousarray(future, f)}


def kernel(**inputs):
    import numpy as np
    import concourse.bacc as bacc
    from concourse.bass_utils import run_bass_kernel_spmd

    nc = bacc.Bacc("TRN2", target_bir_lowering=False, num_devices=1)
    arrays, args = {}, []
    for name, a in [(n, np.ascontiguousarray(inputs[n])) for n in _INS] + list(constants().items()):
        arrays[f"in_{name}"] = a
        args.append(nc.dram_tensor(f"in_{name}", a.shape, mybir.dt.from_np(a.dtype), kind="ExternalInput").ap())
    out = nc.dram_tensor("out_x", (1, SEQ, D), mybir.dt.float32, kind="ExternalOutput").ap()
    program(nc, *args, out)
    r = run_bass_kernel_spmd(nc, [arrays], core_ids=[0])
    return r.results[0]["out_x"]
```
